# Optimizing a Trainium2 kernel written in Bass

```python
import jax, jax.numpy as jnp
from jax import lax
import numpy as np

D_MODEL = 1024
BATCH = 1
SEQ = 256
DEPTH = 2

CHUNK = 64
N_META = 16
A_HEADS = 8
A_HEAD_DIM = 64
A_WIDTH = A_HEADS * A_HEAD_DIM
W_LORA = 64
A_LORA = 64
G_LORA = 128
A_IN = 3 * A_WIDTH + W_LORA + A_LORA + G_LORA
A_SPLITS = [A_WIDTH, 2 * A_WIDTH, 3 * A_WIDTH, 3 * A_WIDTH + W_LORA, 3 * A_WIDTH + W_LORA + A_LORA]
LNX_EPS = 64e-5
B_WIDTH = 512
CONV_WIDTH = 31
C_WIDTH = 512
POOL_WINDOWS = (2, 4, 8, 16)
C_GROUPS = len(POOL_WINDOWS)
C_GROUP_DIM = C_WIDTH // C_GROUPS
N_BRANCH = 3
IN_WIDTH = A_IN + 2 * B_WIDTH + C_WIDTH + N_BRANCH * D_MODEL
IN_SPLITS = [A_IN, A_IN + 2 * B_WIDTH, A_IN + 2 * B_WIDTH + C_WIDTH]
D_FF = 2816
N_EXPERTS = 8
TOP_K = 2
MOE_BLOCK = 256
N_DENSE = (DEPTH + 1) // 2
N_MOE = DEPTH // 2
RMS_EPS = 1e-6
LN_EPS = 1e-5

kernel_name = 'hybrid_stream_encoder_block'

def rmsnorm(x, g):
    xf = x.astype(jnp.float32)
    y = xf * lax.rsqrt(jnp.mean(xf * xf, -1, keepdims=True) + RMS_EPS)
    return (y * g.astype(jnp.float32)).astype(x.dtype)

def shift_one(z):
    return jnp.pad(z, ((0, 0), (1, 0), (0, 0)))[:, :-1]

def _wkv_step(S, inp):
    r, dec, k, v, a_vec, b_vec = inp
    Sa = jnp.einsum('bhvk,bhk->bhv', S, a_vec)
    S = S * dec[:, :, None, :] + Sa[..., None] * b_vec[:, :, None, :] + v[..., None] * k[:, :, None, :]
    return S, jnp.einsum('bhvk,bhk->bhv', S, r)

def _wkv_scan(S, seq):
    return lax.scan(_wkv_step, S, seq)

def wkv7(r, dec, k, v, a_vec, b_vec):
    seq = tuple(jnp.moveaxis(t.astype(jnp.float32), 1, 0) for t in (r, dec, k, v, a_vec, b_vec))
    bn, nh, nd = r.shape[0], r.shape[2], r.shape[3]
    S0 = jnp.zeros((bn, nh, nd, nd), jnp.float32)
    S1, y_meta = _wkv_scan(S0, tuple(t[:N_META] for t in seq))
    frames = tuple(t[N_META:].reshape((-1, CHUNK) + t.shape[1:]) for t in seq)
    _, y_frames = lax.scan(_wkv_scan, S1, frames)
    y = jnp.concatenate([y_meta, y_frames.reshape((-1,) + y_meta.shape[1:])], 0)
    return jnp.moveaxis(y, 0, 1)

def rwkv7_mixer(z, mu, w0, w2, a0, a2, g2, k_k, k_a, r_k, lnx_w, lnx_b):
    bn, L, _ = z.shape
    z = z + (shift_one(z) - z) * mu
    r, k, v, wd, ad, gd = jnp.split(z, A_SPLITS, -1)
    w_log = -jax.nn.softplus(-(w0 + jnp.tanh(wd) @ w2)) - 0.5
    dec = jnp.exp(-jnp.exp(w_log.astype(jnp.float32)))
    a = jax.nn.sigmoid(a0 + ad @ a2)
    g = jax.nn.sigmoid(gd) @ g2
    hs = lambda t: t.reshape(bn, L, A_HEADS, A_HEAD_DIM)
    kk = hs(k * k_k).astype(jnp.float32)
    kk = kk / jnp.maximum(jnp.sqrt(jnp.sum(kk * kk, -1, keepdims=True)), 1e-12)
    k = k * (1.0 + (a - 1.0) * k_a)
    r_h, k_h, v_h, a_h = hs(r), hs(k), hs(v), hs(a)
    y = wkv7(r_h, hs(dec), k_h, v_h, -kk, kk * a_h.astype(jnp.float32))
    mean = jnp.mean(y, -1, keepdims=True)
    var = jnp.mean(jnp.square(y - mean), -1, keepdims=True)
    y = ((y - mean) * lax.rsqrt(var + LNX_EPS)).reshape(bn, L, A_WIDTH)
    y = y * lnx_w.astype(jnp.float32) + lnx_b.astype(jnp.float32)
    bonus = jnp.sum((r_h * k_h * r_k).astype(jnp.float32), -1, keepdims=True) * v_h.astype(jnp.float32)
    y = (y + bonus.reshape(bn, L, A_WIDTH)) * g.astype(jnp.float32)
    return y.astype(z.dtype)

def conformer_conv(z, conv_w, conv_b, ln_g, ln_b):
    c = z[..., :B_WIDTH] * jax.nn.sigmoid(z[..., B_WIDTH:])
    c = lax.conv_general_dilated(c, conv_w.astype(c.dtype), window_strides=(1,),
                                 padding=[(CONV_WIDTH - 1, 0)],
                                 dimension_numbers=('NWC', 'WIO', 'NWC'),
                                 feature_group_count=B_WIDTH) + conv_b
    cf = c.astype(jnp.float32)
    mean = jnp.mean(cf, -1, keepdims=True)
    var = jnp.mean(jnp.square(cf - mean), -1, keepdims=True)
    cf = (cf - mean) * lax.rsqrt(var + LN_EPS) * ln_g.astype(jnp.float32) + ln_b.astype(jnp.float32)
    return jax.nn.silu(cf).astype(z.dtype)

def multiscale_pool(z, pool_w, pool_scale):
    bn, L, _ = z.shape
    zg = z.reshape(bn, L, C_GROUPS, C_GROUP_DIM).astype(jnp.float32)
    cs = jnp.cumsum(zg, axis=1)
    pos = jnp.arange(1, L + 1, dtype=jnp.float32)
    means = []
    for j, w in enumerate(POOL_WINDOWS):
        c = cs[:, :, j]
        prev = jnp.pad(c, ((0, 0), (w, 0), (0, 0)))[:, :L]
        means.append((c - prev) / jnp.minimum(pos, w)[None, :, None])
    pooled = (jnp.stack(means, 2) - zg).astype(z.dtype)
    y = jnp.einsum('blgc,gcd->blgd', pooled, pool_w).reshape(bn, L, C_WIDTH)
    return y * pool_scale

def swiglu(h, w_gate, w_up, w_down):
    return (jax.nn.silu(h @ w_gate) * (h @ w_up)) @ w_down

def moe_swiglu(h, router_w, router_b, e_gate, e_up, e_down):
    bn, L, d = h.shape
    t = h.reshape(-1, d)
    T = t.shape[0]
    logits = (t @ router_w).astype(jnp.float32) + router_b.astype(jnp.float32)
    top_l, top_e = lax.top_k(logits, TOP_K)
    gates = jax.nn.softmax(top_l, -1)
    flat_e = top_e.reshape(-1)
    flat_tok = jnp.repeat(jnp.arange(T, dtype=jnp.int32), TOP_K)
    order = jnp.argsort(flat_e)
    se, stok, sg = flat_e[order], flat_tok[order], gates.reshape(-1)[order]
    counts = jnp.bincount(flat_e, length=N_EXPERTS)
    padded = (counts + MOE_BLOCK - 1) // MOE_BLOCK * MOE_BLOCK
    start_sorted = jnp.cumsum(counts) - counts
    pad_end = jnp.cumsum(padded)
    start_pad = pad_end - padded
    dest = start_pad[se] + jnp.arange(T * TOP_K, dtype=jnp.int32) - start_sorted[se]
    n_blocks = (T * TOP_K + N_EXPERTS * (MOE_BLOCK - 1) + MOE_BLOCK - 1) // MOE_BLOCK
    slot_tok = jnp.full((n_blocks * MOE_BLOCK,), T, jnp.int32).at[dest].set(stok)
    block_e = jnp.minimum(jnp.searchsorted(pad_end, jnp.arange(n_blocks) * MOE_BLOCK, side='right'), N_EXPERTS - 1)
    t_pad = jnp.concatenate([t, jnp.zeros((1, d), t.dtype)], 0)

    def run_block(args):
        tok, e = args
        xb = t_pad[tok]
        return swiglu(xb, e_gate[e], e_up[e], e_down[e])

    y_slots = lax.map(run_block, (slot_tok.reshape(n_blocks, MOE_BLOCK), block_e)).reshape(-1, d)
    y = jax.ops.segment_sum(y_slots[dest] * sg[:, None].astype(y_slots.dtype), stok, num_segments=T)
    return y.reshape(bn, L, d)

def setup_inputs(seed: int = 0) -> dict:
    key = jax.random.key(seed)
    ks = iter(jax.random.split(key, 48))
    f32 = jnp.float32
    nrm = lambda shape, scale: scale * jax.random.normal(next(ks), shape, f32)
    return {
        'x': nrm((BATCH, SEQ, D_MODEL), 1.0),
        'meta_tokens': nrm((N_META, D_MODEL), 1.0),
        'mix_norm_g': 1.0 + nrm((DEPTH, D_MODEL), 0.05),
        'w_in': nrm((DEPTH, D_MODEL, IN_WIDTH), D_MODEL ** -0.5),
        'gate_b': nrm((DEPTH, N_BRANCH * D_MODEL), 0.1),
        'a_mu': jax.random.uniform(next(ks), (DEPTH, A_IN), f32),
        'a_w0': -2.0 + nrm((DEPTH, A_WIDTH), 1.0),
        'a_w2': nrm((DEPTH, W_LORA, A_WIDTH), 0.5 * W_LORA ** -0.5),
        'a_a0': nrm((DEPTH, A_WIDTH), 0.5),
        'a_a2': nrm((DEPTH, A_LORA, A_WIDTH), 0.5 * A_LORA ** -0.5),
        'a_g2': nrm((DEPTH, G_LORA, A_WIDTH), G_LORA ** -0.5),
        'a_kk': 0.85 + nrm((DEPTH, A_WIDTH), 0.05),
        'a_ka': 1.0 + nrm((DEPTH, A_WIDTH), 0.05),
        'a_rk': nrm((DEPTH, A_HEADS, A_HEAD_DIM), 0.1),
        'a_lnx_w': 1.0 + nrm((DEPTH, A_WIDTH), 0.05),
        'a_lnx_b': nrm((DEPTH, A_WIDTH), 0.01),
        'b_conv_w': nrm((DEPTH, CONV_WIDTH, 1, B_WIDTH), CONV_WIDTH ** -0.5),
        'b_conv_b': nrm((DEPTH, B_WIDTH), 0.01),
        'b_ln_g': 1.0 + nrm((DEPTH, B_WIDTH), 0.05),
        'b_ln_b': nrm((DEPTH, B_WIDTH), 0.01),
        'c_pool_w': nrm((DEPTH, C_GROUPS, C_GROUP_DIM, C_GROUP_DIM), C_GROUP_DIM ** -0.5),
        'c_scale': 1.0 + nrm((DEPTH, C_WIDTH), 0.05),
        'proj_a': nrm((DEPTH, A_WIDTH, D_MODEL), A_WIDTH ** -0.5),
        'proj_b': nrm((DEPTH, B_WIDTH, D_MODEL), B_WIDTH ** -0.5),
        'proj_c': nrm((DEPTH, C_WIDTH, D_MODEL), C_WIDTH ** -0.5),
        'w_out': nrm((DEPTH, D_MODEL, D_MODEL), 0.5 * D_MODEL ** -0.5),
        'ffn_norm_g': 1.0 + nrm((DEPTH, D_MODEL), 0.05),
        'ffn_gate': nrm((N_DENSE, D_MODEL, D_FF), D_MODEL ** -0.5),
        'ffn_up': nrm((N_DENSE, D_MODEL, D_FF), D_MODEL ** -0.5),
        'ffn_down': nrm((N_DENSE, D_FF, D_MODEL), 0.5 * D_FF ** -0.5),
        'router_w': nrm((N_MOE, D_MODEL, N_EXPERTS), D_MODEL ** -0.5),
        'router_b': nrm((N_MOE, N_EXPERTS), 0.01),
        'exp_gate': nrm((N_MOE, N_EXPERTS, D_MODEL, D_FF), D_MODEL ** -0.5),
        'exp_up': nrm((N_MOE, N_EXPERTS, D_MODEL, D_FF), D_MODEL ** -0.5),
        'exp_down': nrm((N_MOE, N_EXPERTS, D_FF, D_MODEL), 0.5 * D_FF ** -0.5),
        'final_norm_g': 1.0 + nrm((D_MODEL,), 0.05),
    }

def reference(x, meta_tokens, mix_norm_g, w_in, gate_b, a_mu, a_w0, a_w2, a_a0, a_a2, a_g2,
              a_kk, a_ka, a_rk, a_lnx_w, a_lnx_b, b_conv_w, b_conv_b, b_ln_g, b_ln_b,
              c_pool_w, c_scale, proj_a, proj_b, proj_c, w_out, ffn_norm_g, ffn_gate, ffn_up,
              ffn_down, router_w, router_b, exp_gate, exp_up, exp_down, final_norm_g):
    bn = x.shape[0]
    meta = jnp.broadcast_to(meta_tokens[None].astype(x.dtype), (bn, N_META, D_MODEL))
    h = jnp.concatenate([meta, x], 1)
    for i in range(DEPTH):
        n = rmsnorm(h, mix_norm_g[i])
        u = n @ w_in[i]
        z_a, z_b, z_c, z_g = jnp.split(u, IN_SPLITS, -1)
        y_a = rwkv7_mixer(z_a, a_mu[i], a_w0[i], a_w2[i], a_a0[i], a_a2[i], a_g2[i],
                          a_kk[i], a_ka[i], a_rk[i], a_lnx_w[i], a_lnx_b[i])
        y_b = conformer_conv(z_b, b_conv_w[i], b_conv_b[i], b_ln_g[i], b_ln_b[i])
        y_c = multiscale_pool(z_c, c_pool_w[i], c_scale[i])
        g_a, g_b, g_c = jnp.split(jax.nn.sigmoid(z_g + gate_b[i]), N_BRANCH, -1)
        merged = g_a * (y_a @ proj_a[i]) + g_b * (y_b @ proj_b[i]) + g_c * (y_c @ proj_c[i])
        h = h + merged @ w_out[i]
        n = rmsnorm(h, ffn_norm_g[i])
        if i % 2 == 0:
            f = swiglu(n, ffn_gate[i // 2], ffn_up[i // 2], ffn_down[i // 2])
        else:
            f = moe_swiglu(n, router_w[i // 2], router_b[i // 2], exp_gate[i // 2], exp_up[i // 2], exp_down[i // 2])
        h = h + f
    return rmsnorm(h, final_norm_g)[:, N_META:]


_drawn_inputs = setup_inputs


def setup_inputs(seed=0):
    import zlib

    import numpy as np

    out = dict(_drawn_inputs(seed))
    spreads = {}
    factors = {'a_w2': 3.941,
     'a_kk': 118.258,
     'a_ka': 4.682,
     'a_lnx_w': 3.136,
     'a_lnx_b': 26.876,
     'b_conv_b': 6.914,
     'b_ln_g': 2.857,
     'b_ln_b': 20.471,
     'router_b': 10.863,
     'c_scale': 3.589}
    for name, (base, spread) in spreads.items():
        noise = np.random.default_rng([zlib.crc32(name.encode()), seed]).standard_normal(out[name].shape)
        drawn = base * np.exp(spread * noise) if base else spread * noise
        out[name] = __import__('jax').numpy.asarray(drawn.astype(out[name].dtype))
    for name, factor in factors.items():
        out[name] = (out[name] * factor).astype(out[name].dtype)
    return out
```

```python
from contextlib import ExitStack

import numpy as np

import concourse.bass as bass
from concourse import mybir

F32 = mybir.dt.float32
F32R = mybir.dt.float32r
U8 = mybir.dt.uint8
I32 = mybir.dt.int32
ALU = mybir.AluOpType
ACT = mybir.ActivationFunctionType
AX_X = mybir.AxisListType.X

P = 128
D = 1024
KD = D // P
SEQ = 256
META = 16
T = META + SEQ
DEPTH = 2
HD = 64
NPAIR = 4
AW = NPAIR * P
A_TILES, C_TILES, B_TILES = 14, 4, 8
A_IN = A_TILES * P
TAPS = 31
PADC = 16
F = 2816
FT = F // P
E = 8
SLOTS = 128
PASSES = SEQ // SLOTS
FG = F // 256
SPLITS = 3
CHUNKS = [(0, META)] + [(META + i * HD, HD) for i in range(SEQ // HD)]
NCH = len(CHUNKS)
RMS_EPS, LN_EPS, LNX_EPS = 1e-6, 1e-5, 64e-5
DECAY = float(np.exp(-0.5))

COLS = dict(gate_b=(0, 24), w0=(24, 4), a0=(28, 4), mix_g=(32, 8), mu=(40, 14), kk=(54, 4), ka=(58, 4), rk=(62, 4),
            lnx_w=(66, 4), lnx_b=(70, 4), conv_b=(74, 4), b_g=(78, 4), b_b=(82, 4), c_scale=(86, 4), ffn_g=(90, 8))
NPAR = 98

CF = dict(ident=(0, 128), head_mean=(128, 128), d_mean=(256, 128), c_mean=(384, 128), strict64=(512, 128),
          incl64=(640, 64), strict16=(704, 32), incl16=(736, 16), inv_win=(752, 64), before=(816, 128),
          ones=(944, 128), slot=(1072, 128), eps=(1200, 3))
NCF = 1203
CU_SCAN = 0
CU_64 = T * NPAIR
CU_16 = CU_64 + 6 * 2 * 128
NCU = CU_16 + 4 * 2 * 32
ARENA = 33088

RING = 6
ERING = 22
EARLY = 8
UNIT = 1024
Z_ORDER = [12, 13, 4, 5, 6, 7, 0, 1, 2, 3, 8, 9, 10, 11] + [22, 23, 24, 25] + list(range(14, 22))
W_IN_UNITS = 26
MIX_UNITS = W_IN_UNITS + 3 * 4 * 3 + 8
FFN_UNITS = 11 * 4 + FT
MOE_UNIT0 = 2 * MIX_UNITS + FFN_UNITS
assert FFN_UNITS % RING == 0


def constants():
    f = np.zeros((P, NCF), np.float32)
    u = np.zeros((P, NCU), np.float32)

    def put(name, a):
        f[:a.shape[0], CF[name][0]:CF[name][0] + a.shape[1]] = a

    i = np.arange(P)
    put("ident", np.eye(P))
    put("head_mean", (i[:, None] // HD == i[None] // HD) / HD)
    put("d_mean", np.full((P, P), 1 / D))
    put("c_mean", np.full((P, P), 1 / AW))
    for n in (64, 16):
        r = np.arange(2 * n)
        same = r[:, None] // n == r[None] // n
        put(f"strict{n}", same & (r[:, None] < r[None]))
        put(f"incl{n}", r[:, None] % n <= np.arange(n)[None])
        for lv in range(6 if n == 64 else 4):
            b = 1 << lv
            s, t = r[:, None] % n, r[None] % n
            m = same & (s // (2 * b) == t // (2 * b)) & (s // b % 2 == 0) & (t // b % 2 == 1)
            at = (CU_64 if n == 64 else CU_16) + lv * 2 * 2 * n
            u[:2 * n, at:at + 2 * n] = m
            u[:2 * n, at + 2 * n:at + 4 * n] = m.T
    put("inv_win", np.tile(np.concatenate([1.0 / np.minimum(np.arange(1, 17), 2 << j) for j in range(4)])[None], (P, 1)))
    put("before", i[:, None] < i[None])
    put("ones", np.ones((P, P)))
    put("slot", np.tile(i[None], (P, 1)))
    put("eps", np.tile(np.array([RMS_EPS, LN_EPS, LNX_EPS])[None], (P, 1)))
    starts = np.ones(T)
    starts[[o for o, _ in CHUNKS]] = 0
    u[:, CU_SCAN:CU_SCAN + NPAIR * T] = np.tile(starts, NPAIR)[None]
    return f, u


def build(nc, x, meta, w_in, lora, g2, pool_w, params, conv_w, proj_a, proj_b, proj_c, w_out,
          ffn_gate, ffn_up, ffn_down, router_w, router_b, exp_gate, exp_up, exp_down, final_g, const_f, const_u, out):
    ctx = ExitStack()
    with ctx:
        def sb(name, cols, dt=F32):
            return ctx.enter_context(nc.sbuf_tensor(name, [P, cols], dt))

        def sem(name):
            return ctx.enter_context(nc.semaphore(name))

        ps = ctx.enter_context(nc.psum_tensor("ps", [P, 8, 512], F32))

        ring = sb("ring", RING * UNIT)
        cf = sb("cf", NCF)
        cu = sb("cu", NCU, U8)
        par = sb("par", DEPTH * NPAR)
        half = sb("half", 32)
        omka = sb("omka", NPAIR)
        taps = sb("taps", DEPTH * NPAIR * TAPS)
        lora_w = sb("lora_w", AW)
        g2_w = sb("g2_w", AW)
        pool_wt = sb("pool_wt", AW)
        rout_w = sb("rout_w", KD * E)
        rout_b = sb("rout_b", E)
        arena = sb("arena", ARENA)
        split = sb("split", SPLITS * 2 * UNIT + 2 * KD * SLOTS + 2 * 2 * 256, F32R)
        at = [0]

        def take(n):
            v = arena[:, at[0]:at[0] + n]
            at[0] += n
            return v

        hT = take(KD * T).rearrange("p (k t) -> p k t", k=KD)
        nT = take(KD * T).rearrange("p (k t) -> p k t", k=KD)
        mixer_at = at[0]
        stage = arena[:, at[0]:at[0] + NCU]
        za = take(A_TILES * (T + 1)).rearrange("p (j t) -> p j t", j=A_TILES)
        zr, zk, zv = (za[:, 4 * i:4 * i + 4, 1:T + 1] for i in range(3))
        yA, bonus = zr, zk
        chunk_at = at[0]
        region = take(2 * 4608)
        tmp = [region[:, i * NPAIR * T:(i + 1) * NPAIR * T] for i in range(7)]
        tm = [t.rearrange("p (j t) -> p j t", j=NPAIR) for t in tmp]
        merged = region[:, 5 * NPAIR * T:7 * NPAIR * T].rearrange("p (k t) -> p k t", k=KD)
        xt = region[:, 0:3 * D].rearrange("p (i d) -> p i d", i=3)
        bd_a, bd_b, bd_k, bd_v, pair_ar = (take(2 * NPAIR * T) for _ in range(5))
        sq = pair_ar.rearrange("p (k t) -> p k t", k=KD)
        pool1 = pair_ar[:, 0:4 * (T + PADC)].rearrange("p (j t) -> p j t", j=4)
        pool2 = pair_ar[:, 4 * (T + PADC):7 * (T + PADC)].rearrange("p (j t) -> p j t", j=3)
        zc = take(NPAIR * (T + PADC)).rearrange("p (j t) -> p j t", j=NPAIR)
        glu = take(NPAIR * (T + TAPS - 1)).rearrange("p (j t) -> p j t", j=NPAIR)
        yB_flat = take(NPAIR * T)
        yB = yB_flat.rearrange("p (j t) -> p j t", j=NPAIR)
        yC = zc[:, :, PADC:]
        th2 = take(2 * T).rearrange("p (j t) -> p j t", j=2)
        state = take(NPAIR * P).rearrange("p (j v) -> p j v", j=NPAIR)
        chunk_decay = take(NCH * NPAIR).rearrange("p (c j) -> p c j", c=NCH)
        nrm = take(T)
        mixer_end = at[0]

        def cb(b, slot, w, rows, n=1):
            o = b * 4608 + slot * 512
            return region[0:rows, o:o + 4 * w].rearrange("p (j c) -> p j c", j=NPAIR)

        at[0] = mixer_at
        hid_flat = take(FT * T)
        hid = hid_flat.rearrange("p (f t) -> p f t", f=FT)
        fth = take(4 * T).rearrange("p (r t) -> p r t", r=4)
        ftm = take(2 * T).rearrange("p (r t) -> p r t", r=2)
        assert at[0] <= mixer_end

        bd_at = chunk_at + 2 * 4608
        tail_at = bd_at + 5 * 2 * NPAIR * T
        eslots = [arena[:, bd_at + i * UNIT:bd_at + (i + 1) * UNIT] for i in range(EARLY)]
        eslots += [ring[:, u % RING * UNIT:(u % RING + 1) * UNIT] for u in range(MOE_UNIT0, MOE_UNIT0 + RING)]
        for i in range(2 * KD * T // UNIT):
            eslots.append(arena[:, i * UNIT:(i + 1) * UNIT])
        for i in range((mixer_end - tail_at) // UNIT):
            eslots.append(arena[:, tail_at + i * UNIT:tail_at + (i + 1) * UNIT])
        assert EARLY * UNIT <= 4 * 2 * NPAIR * T and len(eslots) >= ERING, len(eslots)
        at[0] = mixer_at
        hid_t = take(F)
        eth = take(2 * 256).rearrange("p (r c) -> p r c", r=2)
        etm = take(2 * 256).rearrange("p (r c) -> p r c", r=2)
        ntok = take(2 * D).rearrange("p (i d) -> p i d", i=2)
        hres = take(2 * D).rearrange("p (i d) -> p i d", i=2)
        ye = take(D)
        pick = take(2 * SLOTS).rearrange("p (i s) -> p i s", i=2)
        pickw = take(2 * SLOTS).rearrange("p (i s) -> p i s", i=2)
        pickT = take(2 * P)
        lg, eq1, eq2, first1, first2, cnt1, lg2, gw, sel, pos0, pos1 = (
            take(2 * E).rearrange("p (i e) -> p i e", i=2) for _ in range(11))
        mx = take(2 * 6).rearrange("p (i c) -> p i c", c=6)
        count_i = take(E)
        fg = take(D)
        ssq = take(4)
        assert at[0] <= bd_at, (at[0], bd_at)
        if len(eslots) < ERING:
            eslots.append(arena[:, at[0]:at[0] + UNIT])

        def parts(o, n, buffers):
            return [[split[:, o + (2 * b + i) * n:o + (2 * b + i + 1) * n] for i in range(2)] for b in range(buffers)]

        wsplit = parts(0, UNIT, SPLITS)
        xe_s = parts(SPLITS * 2 * UNIT, KD * SLOTS, 1)[0]
        hid_s = parts(SPLITS * 2 * UNIT + 2 * KD * SLOTS, 256, 2)
        YBANK = {(0, 0): 4, (1, 0): 5, (0, 1): 2, (1, 1): 3}

        def c_(name, rows=P):
            return cf[0:rows, CF[name][0]:CF[name][0] + CF[name][1]]

        def p_(l, name, j=None):
            o, w = COLS[name]
            o += l * NPAR
            return par[:, o:o + w] if j is None else par[:, o + j:o + j + 1]

        def wide(ap, n):
            return ap.unsqueeze(2).broadcast_to([ap.shape[0], ap.shape[1], n])

        def block(buf, rows, j, o, n):
            return buf[0:rows, j * 2 * T + 2 * o:j * 2 * T + 2 * o + 2 * n]

        def halves(buf, part, h, o, n, chunks):
            v = buf[part, :].rearrange("p (j c) -> p j c", j=NPAIR)[:, :, 2 * o:2 * o + 2 * n * chunks]
            return v.rearrange("p j (c h n) -> p j c h n", h=2, n=n)[:, :, :, h]

        def cols(v, part, o, n, chunks):
            return v[part, :, o:o + n * chunks].rearrange("p j (c n) -> p j c n", n=n)

        ALLP, LOW, HIGH = slice(0, P), slice(0, HD), slice(HD, P)
        SPANS = [(0, META, 1), (META, HD, NCH - 1)]

        const_in = sem("const_in")
        x_in = sem("x_in")
        small_in = sem("small_in")
        moe_in = sem("moe_in")
        ring_in = [sem(f"ring_in{i}") for i in range(RING)]
        ring_used = sem("ring_used")
        prep_done = sem("prep_done")
        masks_done = sem("masks_done")
        half_done = sem("half_done")
        dve_step = sem("dve_step")
        act_step = sem("act_step")
        xt_ready, xt_taken = sem("xt_ready"), sem("xt_taken")
        h_ready = sem("h_ready")
        sq_done, ssq_ready, n_ready = sem("sq_done"), sem("ssq_ready"), sem("n_ready")
        z_ready, z_taken = sem("z_ready"), sem("z_taken")
        lora_mixed, lora_act = sem("lora_mixed"), sem("lora_act")
        lora_ready, lora_taken = sem("lora_ready"), sem("lora_taken")
        gd_tanh, gd_done = sem("gd_tanh"), sem("gd_done")
        glu_done = sem("glu_done")
        kk_sq, kk_ss = sem("kk_sq"), sem("kk_ss")
        decay_log, decay_exp = sem("decay_log"), sem("decay_exp")
        bonus_in, bonus_ready = sem("bonus_in"), sem("bonus_ready")
        wkv_in = sem("wkv_in")
        pooled, pool_ready, pool_taken = sem("pooled"), sem("pool_ready"), sem("pool_taken")
        merge_ready, gate_done, merge_taken = sem("merge_ready"), sem("gate_done"), sem("merge_taken")
        out_ready = sem("out_ready")
        w_prod, w_dve, w_act = sem("w_prod"), sem("w_dve"), sem("w_act")
        x_init = sem("x_init")
        w_id = sem("w_id")
        conv_done = sem("conv_done")
        stat_ready = sem("stat_ready")
        stat_cen, stat_sq = sem("stat_cen"), sem("stat_sq")
        kk_floor = sem("kk_floor")
        root_done = sem("root_done")
        yb_lin, yb_tanh = sem("yb_lin"), sem("yb_tanh")
        yb_done, ya_done = sem("yb_done"), sem("ya_done")
        g_ready = sem("g_ready")
        hu_ready, hu_gate, hu_taken = sem("hu_ready"), sem("hu_gate"), sem("hu_taken")
        down_ready, down_taken = sem("down_ready"), sem("down_taken")
        tr_ready, tr_taken, res_taken = sem("tr_ready"), sem("tr_taken"), sem("res_taken")
        logit_ready, gap_ready, gap_exp = sem("logit_ready"), sem("gap_ready"), sem("gap_exp")
        sel_ready, pos_ready, route_done = sem("sel_ready"), sem("pos_ready"), sem("route_done")
        pick_ready, gather_ready, gather_taken = sem("pick_ready"), sem("gather_ready"), sem("gather_taken")
        moe_step = sem("moe_step")
        ering_in = [sem(f"ering_in{i}") for i in range(ERING)]
        w_hi = sem("w_hi")
        split_used = sem("split_used")
        egate_tanh, ehid_done = sem("egate_tanh"), sem("ehid_done")
        ehid_tr, ehid_hi, ehid_lo = sem("ehid_tr"), sem("ehid_hi"), sem("ehid_lo")
        xe_lo_done = sem("xe_lo_done")
        y_ready, y_taken = sem("y_ready"), sem("y_taken")
        scat_ready, scat_taken = sem("scat_ready"), sem("scat_taken")
        fin_sq, fin_done, out_sent = sem("fin_sq"), sem("fin_done"), sem("out_sent")

        CONST_DMAS = 4

        def c0_of(l):
            return 0 if l < DEPTH - 1 else META

        def levels(n):
            return 5 if n == HD else 3

        GROUPS = [[0, 1], [2, 3], [4]]

        def wkv_schedule():
            order = []
            for grp in GROUPS:
                for c in grp:
                    order += [(c, g) for g in ("M1", "M2", "TB", "TK")]
                for c in grp:
                    order += [(c, g) for g in ("TV", "TN")]
                for lv in range(1, 6):
                    for c in grp:
                        if lv <= levels(CHUNKS[c][1]):
                            order += [(c, f"W{lv}")]
                    for c in grp:
                        if lv <= levels(CHUNKS[c][1]):
                            order += [(c, f"P{lv}")]
                            if lv < levels(CHUNKS[c][1]):
                                order += [(c, f"Q{lv}")]
                for c in grp:
                    order += [(c, g) for g in ("R", "U", "Y", "S")]
            return order

        ORDER = wkv_schedule()
        prod_at = {key: i + 1 for i, key in enumerate(ORDER)}

        def taker(g):
            return "act" if g in ("TB", "TK", "TV", "TN", "R", "U", "Y") or g[0] == "W" else "dve"

        act_at, dve_at = {}, {}
        for key in ORDER:
            d = act_at if taker(key[1]) == "act" else dve_at
            d[key] = len(d) + 1

        def wkv_count(l, c, g):
            return l * len(ORDER) + prod_at[(c, g)]

        def taken(eng, l, c, g):
            if taker(g) == "act":
                eng.wait_ge(w_act, l * len(act_at) + act_at[(c, g)])
            else:
                eng.wait_ge(w_dve, l * len(dve_at) + dve_at[(c, g)])

        BANK = {"M1": 0, "M2": 1, "TB": 2, "TK": 3, "TV": 0, "TN": 1, "W": 2, "P": 3, "Q": 0, "R": 1, "U": 2, "Y": 3, "S": 0}

        def kind_of(g):
            return g[0] if g[0] in "WPQ" else g

        def before_in_bank(c, g):
            seq = [k for k in ORDER if k[0] % 2 == c % 2]
            for k in reversed(seq[:seq.index((c, g))]):
                if BANK[kind_of(k[1])] == BANK[kind_of(g)]:
                    return k
            return None

        def mr(b, which, rows):
            at_ = b * 4608 + S_MR * 512 + which * 256
            return region[0:rows, at_:at_ + 2 * rows].rearrange("p (j c) -> p j c", j=NPAIR)

        S_W, S_NT, S_X, S_XT, S_MAK, S_MR, S_V, S_B, S_K = range(9)


        blk = ctx.enter_context(nc.Block())

        @blk.sync
        def _(sp):
            def slot(u):
                return ring[:, (u % RING) * UNIT:(u % RING + 1) * UNIT]

            def unit(u, shape, src, n=0):
                if not isinstance(n, int) or u >= RING:
                    sp.wait_ge(ring_used, u - RING + 1 + n * FFN_UNITS)
                dst = slot(u) if shape is None else slot(u).rearrange("p (k c) -> p k c", k=shape)
                sp.dma_start(dst, src).then_inc(ring_in[u % RING], 16)

            def columns(u, w, c, n=0):
                v = w.rearrange("(k p) c -> p k c", p=P)
                for h in range(2):
                    unit(u + h, 4, v[:, 4 * h:4 * h + 4, c:c + 256], n)

            def swiglu_units(u, wg, wu, wd, n=0):
                for g in range(FT // 2):
                    columns(u, wg, 256 * g, n)
                    columns(u + 2, wu, 256 * g, n)
                    u += 4
                for ft in range(FT):
                    unit(u, None, wd[ft * P:(ft + 1) * P, :], n)
                    u += 1

            u = 0
            for l in range(DEPTH):
                for j in Z_ORDER[::2]:
                    columns(u, w_in[l], j * P)
                    u += 2
                for b, pr in ((2, proj_c), (1, proj_b), (0, proj_a)):
                    for i in range(4):
                        unit(u, 4, pr[l].rearrange("(k p) c -> p k c", p=P)[:, :, 256 * i:256 * i + 256])
                        columns(u + 1, w_in[l], (A_TILES + B_TILES + C_TILES + KD * b) * P + 256 * i)
                        u += 3
                for i in range(4):
                    columns(u, w_out[l], 256 * i)
                    u += 2
                if l == 0:
                    swiglu_units(u, ffn_gate[0], ffn_up[0], ffn_down[0])
                    u += FFN_UNITS
            assert u == MOE_UNIT0
            wg, wu, wd = (w.rearrange("a e r c -> (a e) r c") for w in (exp_gate, exp_up, exp_down))

            def expert_units(e, n):
                g_, u_, d_ = (w[bass.ds(e, 1)].rearrange("a r c -> (a r) c") for w in (wg, wu, wd))
                gv, uv = (w.rearrange("(k p) c -> p k c", p=P) for w in (g_, u_))
                for i in range(FFN_UNITS):
                    if not isinstance(n, int) or i >= ERING:
                        sp.wait_ge(ring_used, MOE_UNIT0 + i - ERING + 1 + n * FFN_UNITS)
                    elif i < EARLY:
                        sp.wait_ge(w_prod, DEPTH * len(ORDER))
                    elif i < EARLY + RING:
                        sp.wait_ge(ring_used, MOE_UNIT0 + (i - EARLY) - RING + 1)
                    else:
                        sp.wait_ge(tr_ready, 8)
                        sp.wait_ge(logit_ready, 1)
                    dst = eslots[i % ERING]
                    if i < 4 * FG:
                        g, r_ = divmod(i, 4)
                        v, h = ((gv, uv)[r_ // 2], r_ % 2)
                        sp.dma_start(dst.rearrange("p (k c) -> p k c", k=4), v[:, 4 * h:4 * h + 4, 256 * g:256 * g + 256]).then_inc(ering_in[i % ERING], 16)
                    else:
                        ft = i - 4 * FG
                        sp.dma_start(dst, d_[ft * P:(ft + 1) * P, :]).then_inc(ering_in[i % ERING], 16)

            expert_units(0, 0)
            with sp.Fori(1, E) as e:
                expert_units(e, e)
            sp.wait_ge(route_done, 1)
            with sp.register("passes") as passes:
                sp.reg_mov(passes, E)
                for q in range(1, PASSES):
                    with sp.Fori(0, E) as e:
                        count = sp.value_load(count_i[0:1, bass.ds(e, 1)].bitcast(I32))
                        with sp.If(count > q * SLOTS):
                            expert_units(e, sp.snap(passes))
                            sp.reg_add(passes, passes, 1)
            sp.wait_ge(fin_done, 2)
            for i in range(2):
                sp.dma_start(out[0, i * P:(i + 1) * P, :], ntok[:, i, :]).then_inc(out_sent, 16)
            sp.wait_ge(out_sent, 32)

        @blk.gpsimd
        def _(pool):
            pool.wait_ge(const_in, 16 * CONST_DMAS)
            pool.tensor_copy(cu[:, :], stage).then_inc(masks_done, 1)
            pool.wait_ge(masks_done, 1)
            pool.memset(za[:, :, 0:1], 0.0)
            pool.memset(zc[:, :, 0:PADC], 0.0)
            pool.memset(glu[:, :, 0:TAPS - 1], 0.0)
            for v in (bd_a, bd_b, bd_k, bd_v):
                pool.memset(v, 0.0)
            pool.memset(state, 0.0).then_inc(prep_done, 1)

            def small(l):
                pool.dma_start(lora_w[:, :], lora[l]).then_inc(small_in, 16)
                pool.dma_start(g2_w[:, :], g2[l]).then_inc(small_in, 16)
                pool.dma_start(pool_wt[:, :].rearrange("p (j d) -> p j d", j=NPAIR),
                               pool_w[l].rearrange("j c d -> c j d")).then_inc(small_in, 16)
            small(0)
            pool.dma_start(rout_w[:, :].rearrange("p (k e) -> p k e", e=E),
                           router_w[0].rearrange("(k p) e -> p k e", p=P)).then_inc(moe_in, 16)
            pool.dma_start(rout_b[:, :], router_b[0].partition_broadcast(P)).then_inc(moe_in, 16)
            for l in range(DEPTH):
                if l > 0:
                    pool.wait_ge(h_ready, 2 * l + 1)
                    pool.memset(za[:, :, 0:1], 0.0)
                    pool.memset(zc[:, :, 0:PADC], 0.0)
                    pool.memset(glu[:, :, 0:TAPS - 1], 0.0)
                    for v in (bd_a, bd_b, bd_k, bd_v):
                        pool.memset(v, 0.0)
                    pool.memset(state, 0.0).then_inc(prep_done, 1)
                    small(l)
                for grp in GROUPS:
                    for c in grp:
                        n = CHUNKS[c][1]
                        if c < 2:
                            pool.wait_ge(wkv_in, l + 1)
                        else:
                            pool.wait_ge(w_prod, wkv_count(l, c - 2, "S"))
                        eye = c_("ident", 2 * n)[:, 0:2 * n].unsqueeze(1).broadcast_to([2 * n, NPAIR, 2 * n])
                        pool.tensor_copy(cb(c % 2, 2, 2 * n, 2 * n), eye)
                        pool.tensor_copy(cb(c % 2, 3, 2 * n, 2 * n), eye).then_inc(w_id, 1)
            pool.wait_ge(h_ready, 2 * DEPTH)
            pool.dma_start(fg, final_g.partition_broadcast(P)).then_inc(moe_in, 16)

        @blk.tensor
        def _(pe):
            mm = nc.tensor.matmul
            ident = c_("ident")
            first_of_unit = [None]

            def open_unit(u, n=0):
                if isinstance(n, int):
                    pe.wait_ge(ring_in[u % RING], 16 * (u // RING + 1))
                else:
                    pe.wait_ge(ring_in[u % RING], 16 * (u // RING + 1) + n * (16 * (FFN_UNITS // RING)))
                first_of_unit[0] = u > 0
                return ring[:, (u % RING) * UNIT:(u % RING + 1) * UNIT]

            def mmu(*a, **k):
                ins = mm(*a, **k)
                if first_of_unit[0]:
                    ins.then_inc(ring_used, 1)
                first_of_unit[0] = False
                return ins

            def column_pair(u, outs, rhs, n=0):
                for h in range(2):
                    w = open_unit(u + h, n).rearrange("p (k c) -> p k c", k=4)
                    for i, o in enumerate(outs):
                        for k in range(4):
                            last = mmu(o, w[:, k, i * P:(i + 1) * P], rhs(4 * h + k),
                                       start=(h == 0 and k == 0), stop=(h == 1 and k == 3))
                        if h == 1:
                            yield i, last

            def ssq(m, c0):
                pe.wait_ge(sq_done, m + 1)
                for k in range(KD):
                    last = mm(ps[:, 7, 0:T - c0], c_("d_mean"), sq[:, k, c0:T], start=(k == 0), stop=(k == KD - 1))
                last.then_inc(ssq_ready, 1)

            pe.wait_ge(const_in, 16 * CONST_DMAS)
            pe.wait_ge(x_in, 48)
            for i, (o, n) in enumerate(((0, META), (META, P), (META + P, P))):
                for h in range(2):
                    for k in range(4):
                        last = nc.tensor.transpose(ps[:, 2 * i + h, k * P:k * P + n], xt[0:n, i, (4 * h + k) * P:(4 * h + k + 1) * P],
                                                   ident[0:n, 0:n])
                    last.then_inc(xt_ready, 1)

            u = 0
            for l in range(DEPTH):
                c0 = c0_of(l)
                ssq(2 * l, 0)
                seq = 0
                if l == 0:
                    pe.wait_ge(xt_taken, 5)
                for g in range(13):
                    outs = [ps[:, (seq + i) % 4, 0:T] for i in range(2)]
                    if g >= 2:
                        pe.wait_ge(z_taken, 26 * l + seq - 2)
                    if g == 0:
                        pe.wait_ge(n_ready, (2 * l + 1) * KD)
                    for i, last in column_pair(u, outs, lambda k: nT[:, k, :]):
                        last.then_inc(z_ready, 1)
                    u += 2
                    seq += 2
                    if g == 3:
                        pe.wait_ge(small_in, 48 * (l + 1))
                        pe.wait_ge(lora_act, l + 1)
                        for j in range(NPAIR):
                            last = mm(ps[:, 4 + j, 0:T], lora_w[0:HD, j * P:(j + 1) * P], th2[0:HD, 0, :], start=True, stop=True)
                        last.then_inc(lora_ready, 1)
                    if g == 4:
                        pe.wait_ge(lora_mixed, l + 1)
                        pe.wait_ge(lora_taken, 2 * l + 1)
                        for j in range(NPAIR):
                            last = mm(ps[:, 4 + j, 0:T], lora_w[HD:P, j * P:(j + 1) * P], za[HD:P, 12, 1:T + 1], start=True, stop=True)
                        last.then_inc(lora_ready, 1)
                    if g == 7:
                        pe.wait_ge(kk_sq, l + 1)
                        pe.wait_ge(lora_taken, 2 * l + 2)
                        for j in range(NPAIR):
                            last = mm(ps[:, 4 + j, 0:T], c_("head_mean"), tm[5][:, j, :], start=True, stop=True)
                        last.then_inc(kk_ss, 1)
                pe.wait_ge(pooled, l + 1)
                pe.wait_ge(z_taken, 26 * (l + 1))
                for j in range(NPAIR):
                    last = mm(ps[:, j, 0:T], pool_wt[:, j * P:(j + 1) * P], zc[:, j, PADC:], start=True, stop=True)
                last.then_inc(pool_ready, 1)
                pe.wait_ge(bonus_in, l + 1)
                for j in range(NPAIR):
                    last = mm(ps[:, 4 + j, 0:T], c_("head_mean"), tm[5][:, j, :], start=True, stop=True)
                last.then_inc(bonus_ready, 1)

                pe.wait_ge(wkv_in, l + 1)
                pe.wait_ge(pool_taken, l + 1)
                pe.wait_ge(prep_done, l + 1)
                for c, g in ORDER:
                    o, n = CHUNKS[c]
                    b = c % 2
                    rows = 2 * n
                    kind = kind_of(g)
                    prev = before_in_bank(c, g)
                    if prev is not None:
                        taken(pe, l, *prev)
                    bank = ps[:, 4 * b + BANK[kind], :]
                    X, XT, NT, W = (cb(b, s, rows, rows) for s in (S_X, S_XT, S_NT, S_W))
                    V, B_, K_ = (cb(b, s, P, rows) for s in (S_V, S_B, S_K))
                    MAK = cb(b, S_MAK, rows, rows)
                    MRB, MRK = mr(b, 0, rows), mr(b, 1, rows)
                    R1, U = cb(b, S_XT, P, rows), cb(b, S_W, P, rows)
                    if g == "TN":
                        taken(pe, l, c, "M1")
                    elif kind == "W":
                        if g == "W1":
                            taken(pe, l, c, "TN")
                            pe.wait_ge(x_init, l * NCH + c + 1)
                        else:
                            taken(pe, l, c, f"P{int(g[1:]) - 1}")
                    elif kind == "P":
                        taken(pe, l, c, "W" + g[1:])
                        if g != "P1":
                            taken(pe, l, c, f"Q{int(g[1:]) - 1}")
                    elif g == "R":
                        taken(pe, l, c, "TV")
                        taken(pe, l, c, "M2")
                        if c > 0:
                            taken(pe, l, c - 1, "S")
                    elif g == "U":
                        taken(pe, l, c, "R")
                        taken(pe, l, c, f"P{levels(n)}")
                    elif g == "Y":
                        taken(pe, l, c, "U")
                    elif g == "S":
                        taken(pe, l, c, "TK")
                    for j in range(NPAIR):
                        if g == "M1":
                            last = mm(bank[0:rows, j * rows:(j + 1) * rows], block(bd_b, P, j, o, n), block(pair_ar, P, j, o, n), start=True, stop=True)
                        elif g == "M2":
                            last = mm(bank[0:rows, j * rows:(j + 1) * rows], block(bd_k, P, j, o, n), block(pair_ar, P, j, o, n), start=True, stop=True)
                        elif g in ("TB", "TK", "TV"):
                            src = {"TB": bd_b, "TK": bd_k, "TV": bd_v}[g]
                            last = nc.tensor.transpose(bank[0:rows, j * P:(j + 1) * P], block(src, P, j, o, n), ident)
                        elif g == "TN":
                            last = nc.tensor.transpose(bank[0:rows, j * rows:(j + 1) * rows], W[:, j, :], c_("ident", rows)[:, 0:rows])
                        elif kind == "W":
                            last = mm(bank[0:rows, j * rows:(j + 1) * rows], NT[:, j, :], X[:, j, :], start=True, stop=True)
                        elif kind == "P":
                            last = mm(bank[0:rows, j * rows:(j + 1) * rows], XT[:, j, :], W[:, j, :], start=True, stop=True)
                        elif kind == "Q":
                            last = mm(bank[0:rows, j * rows:(j + 1) * rows], W[:, j, :], XT[:, j, :], start=True, stop=True)
                        elif g == "R":
                            if c > 0:
                                mm(bank[0:rows, j * P:(j + 1) * P], block(bd_a, P, j, o, n), state[:, j, :], start=True, stop=False)
                            last = mm(bank[0:rows, j * P:(j + 1) * P], MAK[:, j, :], V[:, j, :], start=(c == 0), stop=True)
                        elif g == "U":
                            last = mm(bank[0:rows, j * P:(j + 1) * P], X[:, j, :], R1[:, j, :], start=True, stop=True)
                        elif g == "Y":
                            dst = bank[:, j * n:(j + 1) * n]
                            if c > 0:
                                mm(dst, state[:, j, :], block(pair_ar, P, j, o, n)[:, n:2 * n], start=True, stop=False)
                            mm(dst, U[:, j, :], MRB[:, j, :], start=(c == 0), stop=False)
                            last = mm(dst, V[:, j, :], MRK[:, j, :], start=False, stop=True)
                        else:
                            mm(bank[:, j * P:(j + 1) * P], B_[:, j, :], U[:, j, :], start=True, stop=False)
                            last = mm(bank[:, j * P:(j + 1) * P], K_[:, j, :], V[:, j, :], start=False, stop=True)
                    last.then_inc(w_prod, 1)
                for b in range(2):
                    for g in ("R", "U", "Y", "S"):
                        taken(pe, l, NCH - 1 - b, g)

                merge_i = 0
                for b, y in ((2, yC), (1, yB), (0, yA)):
                    if b == 1:
                        pe.wait_ge(yb_done, l + 1)
                    if b == 0:
                        pe.wait_ge(ya_done, l + 1)
                    for i in range(4):
                        if b == 2 and i == 0:
                            for j in range(NPAIR):
                                last = mm(ps[:, 4 + j, 0:T], c_("head_mean"), yA[:, j, :], start=True, stop=True)
                            last.then_inc(stat_ready, 1)
                        if b == 2 and i == 1:
                            pe.wait_ge(conv_done, l + 1)
                            pe.wait_ge(stat_cen, 2 * l + 1)
                            for j in range(NPAIR):
                                last = mm(ps[:, 4, 0:T], c_("c_mean"), yB[:, j, :], start=(j == 0), stop=(j == NPAIR - 1))
                            last.then_inc(stat_ready, 1)
                        if b == 2 and i == 2:
                            pe.wait_ge(stat_sq, 2 * l + 1)
                            pe.wait_ge(stat_cen, 2 * l + 2)
                            for j in range(NPAIR):
                                last = mm(ps[:, 4 + j, 0:T], c_("head_mean"), tm[0][:, j, :], start=True, stop=True)
                            last.then_inc(stat_ready, 1)
                        if b == 2 and i == 3:
                            pe.wait_ge(stat_sq, 2 * l + 2)
                            pe.wait_ge(root_done, 5 * l + 3)
                            for j in range(NPAIR):
                                last = mm(ps[:, 4, 0:T], c_("c_mean"), tm[1][:, j, :], start=(j == 0), stop=(j == NPAIR - 1))
                            last.then_inc(stat_ready, 1)
                        if b == 1 and i == 0:
                            pe.wait_ge(root_done, 5 * l + 4)
                            pe.wait_ge(gd_done, l + 1)
                            for j in range(NPAIR):
                                last = mm(ps[:, 4 + j, 0:T], g2_w[:, j * P:(j + 1) * P], za[:, 13, 1:T + 1], start=True, stop=True)
                            last.then_inc(g_ready, 1)
                        if merge_i >= 1:
                            pe.wait_ge(merge_taken, 24 * l + 2 * merge_i)
                        w = open_unit(u).rearrange("p (k c) -> p k c", k=NPAIR)
                        for t in range(2):
                            for k in range(NPAIR):
                                mmu(ps[:, 2 * t, 0:T - c0], w[:, k, t * P:(t + 1) * P], y[:, k, c0:T], start=(k == 0), stop=(k == NPAIR - 1))
                        for t, last in column_pair(u + 1, [ps[:, 1, 0:T - c0], ps[:, 3, 0:T - c0]], lambda k: nT[:, k, c0:T]):
                            last.then_inc(merge_ready, 1)
                        u += 3
                        merge_i += 1
                pe.wait_ge(merge_taken, 24 * (l + 1))
                for i in range(4):
                    for t, last in column_pair(u, [ps[:, 2 * i, 0:T - c0], ps[:, 2 * i + 1, 0:T - c0]], lambda k: merged[:, k, c0:T]):
                        last.then_inc(out_ready, 1)
                    u += 2
                pe.wait_ge(h_ready, 2 * l + 2)
                ssq(2 * l + 1, c0)
                pe.wait_ge(n_ready, (2 * l + 2) * KD)
                if l == 0:
                    for g in range(FT // 2):
                        b4 = 4 * (g % 2)
                        if g >= 2:
                            pe.wait_ge(hu_taken, 2 * (g - 1))
                        for t, last in column_pair(u, [ps[:, b4, 0:T], ps[:, b4 + 1, 0:T]], lambda k: nT[:, k, :]):
                            pass
                        for t, last in column_pair(u + 2, [ps[:, b4 + 2, 0:T], ps[:, b4 + 3, 0:T]], lambda k: nT[:, k, :]):
                            last.then_inc(hu_ready, 1)
                        u += 4
                    pe.wait_ge(hu_taken, FT)
                    for ft in range(FT):
                        w = open_unit(u)
                        for k in range(KD):
                            last = mmu(ps[:, k, 0:T], w[:, k * P:(k + 1) * P], hid[:, ft, :], start=(ft == 0), stop=(ft == FT - 1))
                        u += 1
                    last.then_inc(down_ready, 1)

            N = SEQ
            for i, src in enumerate((nT, hT)):
                for tt in range(2):
                    for h in range(2):
                        for k in range(4):
                            last = nc.tensor.transpose(ps[:, 4 * i + 2 * tt + h, k * P:(k + 1) * P],
                                                       src[:, 4 * h + k, META + tt * P:META + (tt + 1) * P], ident)
                            if (i, tt, h, k) == (0, 0, 0, 0):
                                last.then_inc(ring_used, 1)
                            if (i, tt, h, k) == (0, 0, 0, 1):
                                last.then_inc(split_used, SPLITS)
                        last.then_inc(tr_ready, 1)
            pe.wait_ge(moe_in, 48)
            pe.wait_ge(tr_taken, 4)
            pe.wait_ge(res_taken, 4)
            for tt in range(2):
                for k in range(KD):
                    last = mm(ps[:, 0, tt * E:(tt + 1) * E], nT[:, k, META + tt * P:META + (tt + 1) * P],
                              rout_w[:, k * E:(k + 1) * E], start=(k == 0), stop=(k == KD - 1))
            last.then_inc(logit_ready, 1)
            pe.wait_ge(sel_ready, 1)
            mm(ps[:, 1, 0:E], c_("before"), sel[:, 0, :], start=True, stop=True)
            mm(ps[:, 1, E:2 * E], c_("ones"), sel[:, 0, :], start=True, stop=False)
            mm(ps[:, 1, E:2 * E], c_("before"), sel[:, 1, :], start=False, stop=True)
            mm(ps[:, 1, 2 * E:3 * E], c_("ones"), sel[:, 0, :], start=True, stop=False)
            mm(ps[:, 1, 2 * E:3 * E], c_("ones"), sel[:, 1, :], start=False, stop=True).then_inc(pos_ready, 1)
            pe.wait_ge(route_done, 1)

            def expert_pass(n):
                pe.wait_ge(pick_ready, n + 1)
                for tt in range(2):
                    last = nc.tensor.transpose(ps[:, 6, tt * P:(tt + 1) * P], pickw[:, tt, :], ident)
                last.then_inc(gather_ready, 1)
                for h in range(2):
                    for k in range(4):
                        for tt in range(2):
                            last = mm(ps[:, 4 + h, k * P:(k + 1) * P], ntok[:, tt, (4 * h + k) * P:(4 * h + k + 1) * P],
                                      pick[:, tt, :], start=(tt == 0), stop=(tt == 1))
                    last.then_inc(gather_ready, 1)
                xh, xl = xe_s

                def split_unit(i):
                    pe.wait_ge(ring_used, n * FFN_UNITS + MOE_UNIT0 + i + 1)
                    return wsplit[i % SPLITS]

                def hid_transpose(d):
                    pe.wait_ge(ehid_done, n * FG + d + 1)
                    if d >= 2:
                        pe.wait_ge(ehid_lo, n * FG + d - 1)
                    for t in range(2):
                        last = nc.tensor.transpose(ps[:, 2 + d % 2, t * P:(t + 1) * P], hid_t[:, (2 * d + t) * P:(2 * d + t + 1) * P], ident)
                    last.then_inc(ehid_tr, 1)

                for i in range(4 * FG):
                    g, (m, h) = i // 4, divmod(i % 4, 2)
                    if i == 4 * (FG - 1):
                        hid_transpose(0)
                    if i % 4 == 0 and g >= 2:
                        pe.wait_ge(ehid_done, n * FG + g - 1)
                    wh, wl = split_unit(i)
                    if i < 2:
                        pe.wait_ge(xe_lo_done, n * 2 + 1 + h)
                    dst = ps[:, 4 * m + g % 2, 0:256]
                    for k in range(4):
                        x_, c = slice((4 * h + k) * SLOTS, (4 * h + k + 1) * SLOTS), slice(k * 256, (k + 1) * 256)
                        mm(dst, xh[:, x_], wh[:, c], start=(h == 0 and k == 0), stop=False)
                        mm(dst, xh[:, x_], wl[:, c], start=False, stop=False)
                        last = mm(dst, xl[:, x_], wh[:, c], start=False, stop=(h == 1 and k == 3))
                    last.then_inc(split_used, 1)
                for ft in range(FT):
                    d = ft // 2
                    if ft % 2 == 0:
                        if d + 1 < FG:
                            hid_transpose(d + 1)
                        pe.wait_ge(ehid_lo, n * FG + d + 1)
                    if ft == 0:
                        pe.wait_ge(gather_taken, n * 3 + 1)
                    wh, wl = split_unit(4 * FG + ft)
                    hh, hl = (v[:, ft % 2 * P:(ft % 2 + 1) * P] for v in hid_s[d % 2])
                    for h in range(2):
                        c = slice(h * 512, (h + 1) * 512)
                        mm(ps[:, 6 + h, :], hh, wh[:, c], start=(ft == 0), stop=False)
                        mm(ps[:, 6 + h, :], hh, wl[:, c], start=False, stop=False)
                        last = mm(ps[:, 6 + h, :], hl, wh[:, c], start=False, stop=(ft == FT - 1))
                    last.then_inc(split_used, 1)
                for h in range(2):
                    pe.wait_ge(y_taken, n * 2 + h + 1)
                    for tt in range(2):
                        mm(ps[:, YBANK[tt, h], :], pickT[:, tt * P:(tt + 1) * P], ye[:, h * 512:(h + 1) * 512],
                           start=True, stop=True).then_inc(scat_ready, 1)
                pe.wait_ge(scat_taken, n * 4 + 4)

            with pe.Fori(0, E) as e:
                expert_pass(e)
            with pe.register("passes") as passes:
                pe.reg_mov(passes, E)
                for q in range(1, PASSES):
                    with pe.Fori(0, E) as e:
                        count = pe.value_load(count_i[0:1, bass.ds(e, 1)].bitcast(I32))
                        with pe.If(count > q * SLOTS):
                            expert_pass(pe.snap(passes))
                            pe.reg_add(passes, passes, 1)

        @blk.scalar
        def _(act):
            af = nc.scalar.activation
            act.dma_start(xt[0:META, 0, :], meta).then_inc(x_in, 16)
            act.dma_start(xt[:, 1, :], x[0, 0:P, :]).then_inc(x_in, 16)
            act.dma_start(xt[:, 2, :], x[0, P:2 * P, :]).then_inc(x_in, 16)
            act.dma_start(cf[:, :], const_f).then_inc(const_in, 16)
            act.dma_start(par[:, :].rearrange("p (l c) -> p l c", l=DEPTH), params.rearrange("l p c -> p l c")).then_inc(const_in, 16)
            act.dma_start(stage, const_u).then_inc(const_in, 16)
            act.dma_start(taps[:, :].rearrange("p (l c) -> p l c", l=DEPTH), conv_w.rearrange("l p c -> p l c")).then_inc(const_in, 16)

            def squares(m, c0):
                act.wait_ge(h_ready, m + 1)
                af(sq[:, :, c0:T], hT[:, :, c0:T], ACT.Square).then_inc(sq_done, 1)
                act.wait_ge(ssq_ready, m + 1)
                af(nrm[:, c0:T], ps[:, 7, 0:T - c0], ACT.Sqrt, bias=eps(0)).then_inc(root_done, 1)

            def eps(i):
                return c_("eps")[:, i:i + 1]

            act.wait_ge(const_in, 16 * CONST_DMAS)

            for l in range(DEPTH):
                c0 = c0_of(l)
                squares(2 * l, 0)
                act.wait_ge(half_done, l + 1)
                act.wait_ge(prep_done, l + 1)
                for s, j in enumerate(Z_ORDER):
                    act.wait_ge(z_ready, 26 * l + s + 1)
                    src = ps[:, s % 4, 0:T]
                    if j < A_TILES:
                        af(za[:, j, 1:T + 1], src, ACT.Copy).then_inc(z_taken, 1)
                    elif j < A_TILES + NPAIR:
                        af(glu[:, j - A_TILES, TAPS - 1:], src, ACT.Copy, scale=0.5).then_inc(z_taken, 1)
                    elif j < A_TILES + B_TILES:
                        af(yB[:, j - A_TILES - NPAIR, :], src, ACT.Tanh, scale=0.5).then_inc(z_taken, 1)
                    else:
                        af(zc[:, j - A_TILES - B_TILES, PADC:], src, ACT.Copy).then_inc(z_taken, 1)
                    if s == 5:
                        act.wait_ge(lora_mixed, l + 1)
                        af(th2[0:HD, 0, :], za[0:HD, 12, 1:T + 1], ACT.Tanh).then_inc(lora_act, 1)
                        af(za[:, 13, 1:T + 1], za[:, 13, 1:T + 1], ACT.Tanh, scale=0.5).then_inc(gd_tanh, 1)
                    if s == 9:
                        act.wait_ge(lora_ready, 2 * l + 1)
                        for j2 in range(NPAIR):
                            last = af(tm[0][:, j2, :], ps[:, 4 + j2, 0:T], ACT.Tanh, scale=0.5, bias=half[:, 24 + j2:25 + j2])
                        last.then_inc(lora_taken, 1)
                    if s == 11:
                        act.wait_ge(lora_ready, 2 * l + 2)
                        for j2 in range(NPAIR):
                            last = af(tm[4][:, j2, :], ps[:, 4 + j2, 0:T], ACT.Tanh, scale=0.5, bias=half[:, 28 + j2:29 + j2])
                        last.then_inc(lora_taken, 1)
                    if s == 17:
                        act.wait_ge(kk_floor, l + 1)
                        af(tmp[5], tmp[5], ACT.Sqrt).then_inc(root_done, 1)
                    if s == 15:
                        act.wait_ge(decay_log, l + 1)
                        af(tmp[2], tmp[2], ACT.Exp).then_inc(decay_exp, 1)
                        af(tmp[0], tmp[1], ACT.Exp, scale=-1.0).then_inc(decay_exp, 1)
                        act.wait_ge(decay_exp, 3 * l + 2)
                        af(tmp[1], tmp[1], ACT.Exp).then_inc(decay_exp, 1)
                act.wait_ge(pool_ready, l + 1)
                for j in range(NPAIR):
                    last = af(yC[:, j, :], ps[:, j, 0:T], ACT.Copy, scale=p_(l, "c_scale", j))
                last.then_inc(pool_taken, 1)

                for c, g in ORDER:
                    if taker(g) != "act":
                        continue
                    o, n = CHUNKS[c]
                    b = c % 2
                    rows = 2 * n
                    kind = kind_of(g)
                    act.wait_ge(w_prod, wkv_count(l, c, g))
                    bank = ps[:, 4 * b + BANK[kind], :]
                    if kind == "W":
                        if g == "W1":
                            act.wait_ge(x_init, l * NCH + c + 1)
                        dst, src = cb(b, S_W, rows, rows), bank[0:rows, 0:4 * rows]
                    elif g == "TN":
                        dst, src = cb(b, S_NT, rows, rows), bank[0:rows, 0:4 * rows]
                    elif g == "Y":
                        dst, src = yA[:, :, o:o + n], bank[:, 0:4 * n]
                    else:
                        slot_ = {"TB": S_B, "TK": S_K, "TV": S_V, "R": S_XT, "U": S_W}[g]
                        dst, src = cb(b, slot_, P, rows), bank[0:rows, :]
                    af(dst, src.rearrange("p (j c) -> p j c", j=NPAIR), ACT.Copy).then_inc(w_act, 1)

                act.wait_ge(stat_cen, 2 * l + 1)
                af(tmp[0], tmp[2], ACT.Square).then_inc(stat_sq, 1)
                act.wait_ge(stat_cen, 2 * l + 2)
                af(tmp[1], tmp[3], ACT.Square).then_inc(stat_sq, 1)

                for i in range(24):
                    if i == 4:
                        act.wait_ge(stat_ready, 4 * l + 3)
                        af(tm[4], ps[:, 4:8, 0:T], ACT.Sqrt, bias=eps(2)).then_inc(root_done, 1)
                    if i == 6:
                        act.wait_ge(stat_ready, 4 * l + 4)
                        af(nrm, ps[:, 4, 0:T], ACT.Sqrt, bias=eps(1)).then_inc(root_done, 1)
                        act.wait_ge(yb_lin, l + 1)
                        af(tmp[1], yB_flat, ACT.Tanh, scale=0.5).then_inc(yb_tanh, 1)
                    act.wait_ge(merge_ready, 24 * l + i + 1)
                    if i >= 2:
                        act.wait_ge(merge_taken, 24 * l + i - 1)
                    b = (2, 1, 0)[i // 8]
                    j = 8 * b + i % 8
                    af(th2[:, i % 2, c0:T], ps[:, 2 * (i % 2) + 1, 0:T - c0], ACT.Tanh, scale=0.5, bias=half[:, j:j + 1]).then_inc(gate_done, 1)
                squares(2 * l + 1, c0)
                if l == 0:
                    for ft in range(FT):
                        act.wait_ge(hu_ready, ft + 1)
                        if ft >= 4:
                            act.wait_ge(hu_taken, ft - 3)
                        af(fth[:, ft % 4, :], ps[:, 4 * (ft // 2 % 2) + ft % 2, 0:T], ACT.Tanh, scale=0.5).then_inc(hu_gate, 1)

            for i in range(4):
                act.wait_ge(tr_ready, i + 1)
                af(ntok[:, i // 2, i % 2 * 512:(i % 2 + 1) * 512], ps[:, i, :], ACT.Copy).then_inc(tr_taken, 1)
            act.wait_ge(gap_ready, 1)
            af(mx[:, :, 3], mx[:, :, 2], ACT.Exp).then_inc(gap_exp, 1)
            act.wait_ge(route_done, 1)

            def expert_pass(n):
                def w_round(i):
                    act.wait_ge(split_used, n * FFN_UNITS + i + 1)
                    act.wait_ge(ering_in[i % ERING], 16 * (i // ERING + 1) + n * (16 * (FFN_UNITS // ERING)))
                    af(wsplit[i % SPLITS][0], eslots[i % ERING], ACT.Copy).then_inc(w_hi, 1)

                w_round(0)
                act.wait_ge(gather_ready, n * 3 + 1)
                af(pickT, ps[:, 6, 0:2 * P], ACT.Copy).then_inc(gather_taken, 1)
                for h in range(2):
                    act.wait_ge(gather_ready, n * 3 + 2 + h)
                    af(xe_s[0][:, h * 512:(h + 1) * 512], ps[:, 4 + h, :], ACT.Copy).then_inc(gather_taken, 1)
                for i in range(1, FFN_UNITS):
                    g, d = (i - 4) // 4, (i - 4 * FG) // 2
                    if i % 4 == 0 and g < FG:
                        act.wait_ge(split_used, n * FFN_UNITS + SPLITS + 4 * g + 2)
                        af(eth[:, g % 2, :], ps[:, g % 2, 0:256], ACT.Tanh, scale=0.5).then_inc(egate_tanh, 1)
                    w_round(i)
                    if d >= 0 and i % 2 == 0:
                        act.wait_ge(ehid_tr, n * FG + d + 1)
                        af(hid_s[d % 2][0], ps[:, 2 + d % 2, 0:256], ACT.Copy).then_inc(ehid_hi, 1)
                act.wait_ge(split_used, n * FFN_UNITS + SPLITS + FFN_UNITS)
                for h in range(2):
                    af(ye[:, h * 512:(h + 1) * 512], ps[:, 6 + h, :], ACT.Copy).then_inc(y_taken, 1)

            with act.Fori(0, E) as e:
                expert_pass(e)
            with act.register("passes") as passes:
                act.reg_mov(passes, E)
                for q in range(1, PASSES):
                    with act.Fori(0, E) as e:
                        count = act.value_load(count_i[0:1, bass.ds(e, 1)].bitcast(I32))
                        with act.If(count > q * SLOTS):
                            expert_pass(act.snap(passes))
                            act.reg_add(passes, passes, 1)
                act.wait_ge(scat_taken, act.snap(passes) * 4)
            for i in range(2):
                af(ye, hres[:, i, :], ACT.Square, accum_out=ssq[:, i:i + 1]).then_inc(fin_sq, 1)
                act.wait_ge(fin_sq, i + 1)
            for i in range(2):
                af(ssq[:, i:i + 1], ssq[:, i:i + 1], ACT.Sqrt, scale=1.0 / D, bias=eps(0)).then_inc(root_done, 1)

        @blk.vector
        def _(dve):
            v = nc.vector
            steps = [0]

            counts = {}
            latest = []

            def mark(semaphore):
                counts[semaphore.name] = counts.get(semaphore.name, 0) + 1
                latest[:] = [semaphore, counts[semaphore.name]]

            def settle():
                dve.wait_ge(*latest)

            def op(ins):
                steps[0] += 1
                ins.then_inc(dve_step, 1)
                mark(dve_step)
                return steps[0]

            def link(ins):
                dve.wait_ge(dve_step, op(ins))

            def norm(m, g, l, c0):
                dve.wait_ge(root_done, 5 * l + (1 if m % 2 == 0 else 5))
                settle()
                link(v.reciprocal(nrm[:, c0:T], nrm[:, c0:T]))
                settle()
                for k in range(KD):
                    v.scalar_tensor_tensor(nT[:, k, c0:T], hT[:, k, c0:T], p_(l, g, k), nrm[:, c0:T], ALU.mult, ALU.mult).then_inc(n_ready, 1)
                    mark(n_ready)

            dve.wait_ge(const_in, 16 * CONST_DMAS)
            for i, (o, n) in enumerate(((0, META), (META, P), (META + P, P))):
                for h in range(2):
                    dve.wait_ge(xt_ready, 2 * i + h + 1)
                    done = h_ready if i == 2 and h == 1 else xt_taken
                    v.tensor_copy(hT[:, 4 * h:4 * h + 4, o:o + n],
                                  ps[:, 2 * i + h, :].rearrange("p (k t) -> p k t", k=4)[:, :, 0:n]).then_inc(done, 1)
                    mark(done)
            dve.wait_ge(h_ready, 1)

            for l in range(DEPTH):
                c0 = c0_of(l)
                settle()
                link(v.tensor_scalar(half[:, :], par[:, l * NPAR:l * NPAR + 32], 0.5, None, ALU.mult))
                settle()
                v.tensor_scalar(omka[:, :], p_(l, "ka"), -1.0, 1.0, ALU.mult, ALU.add).then_inc(half_done, 1)
                mark(half_done)
                norm(2 * l, "mix_g", l, 0)
                dve.wait_ge(half_done, l + 1)

                def mix(tiles, scratch):
                    a, n = tiles[0], len(tiles)
                    settle()
                    link(v.tensor_tensor(scratch[:, 0:n, :], za[:, a:a + n, 0:T], za[:, a:a + n, 1:T + 1], ALU.subtract))
                    settle()
                    for i, j in enumerate(tiles):
                        last = v.scalar_tensor_tensor(za[:, j, 1:T + 1], scratch[:, i, :], p_(l, "mu", j), za[:, j, 1:T + 1], ALU.mult, ALU.add)
                        if j != tiles[-1]:
                            op(last)
                    return last

                dve.wait_ge(z_taken, 26 * l + 2)
                mix([12, 13], tm[6]).then_inc(lora_mixed, 1)
                mark(lora_mixed)
                dve.wait_ge(z_taken, 26 * l + 6)
                link(mix([4, 5, 6, 7], tm[6]))
                settle()
                link(v.tensor_tensor(tm[3], zk, wide(p_(l, "kk"), T), ALU.mult))
                settle()
                v.tensor_tensor(tm[5], tm[3], tm[3], ALU.mult).then_inc(kk_sq, 1)
                mark(kk_sq)
                dve.wait_ge(gd_tanh, l + 1)
                settle()
                v.tensor_scalar(za[:, 13, 1:T + 1], za[:, 13, 1:T + 1], 1.0, 0.5, ALU.add, ALU.mult).then_inc(gd_done, 1)
                mark(gd_done)
                dve.wait_ge(z_taken, 26 * l + 10)
                op(mix([0, 1, 2, 3], tm[6]))
                dve.wait_ge(lora_taken, 2 * l + 1)
                dve.wait_ge(masks_done, 1)
                settle()
                link(v.tensor_scalar(tmp[0], tmp[0], 1.0, -0.5 * DECAY, ALU.add, ALU.mult))
                settle()
                link(v.tensor_tensor_scan(tmp[1], cu[:, CU_SCAN:CU_SCAN + NPAIR * T], tmp[0], 0.0, ALU.mult, ALU.add))
                settle()
                v.tensor_tensor(tmp[2], tmp[1], tmp[0], ALU.subtract).then_inc(decay_log, 1)
                mark(decay_log)
                dve.wait_ge(z_taken, 26 * l + 14)
                op(mix([8, 9, 10, 11], tm[6]))
                dve.wait_ge(z_taken, 26 * l + 18)
                dve.wait_ge(prep_done, l + 1)
                W_ = T + PADC
                settle()
                link(v.tensor_tensor(pool1[:, 0:4, 1:W_], zc[:, 0:4, 1:W_], zc[:, 0:4, 0:W_ - 1], ALU.add))
                settle()
                link(v.tensor_tensor(pool2[:, 0:3, 3:W_], pool1[:, 1:4, 3:W_], pool1[:, 1:4, 1:W_ - 2], ALU.add))
                settle()
                link(v.tensor_tensor(pool1[:, 2:4, 7:W_], pool2[:, 1:3, 7:W_], pool2[:, 1:3, 3:W_ - 4], ALU.add))
                settle()
                link(v.tensor_tensor(pool2[:, 2, 15:W_], pool1[:, 3, 15:W_], pool1[:, 3, 7:W_ - 8], ALU.add))
                sums = [pool1[:, 0], pool2[:, 0], pool1[:, 2], pool2[:, 2]]
                settle()
                for j in range(4):
                    op(v.tensor_tensor(sums[j][:, PADC:2 * PADC], sums[j][:, PADC:2 * PADC], c_("inv_win")[:, 16 * j:16 * j + 16], ALU.mult))
                settle()
                for j in range(4):
                    op(v.scalar_tensor_tensor(zc[:, j, 2 * PADC:], sums[j][:, 2 * PADC:], 1.0 / (2 << j), zc[:, j, 2 * PADC:], ALU.mult, ALU.subtract))
                dve.wait_ge(dve_step, steps[0] - 1)
                settle()
                for j in range(4):
                    last = v.tensor_tensor(zc[:, j, PADC:2 * PADC], sums[j][:, PADC:2 * PADC], zc[:, j, PADC:2 * PADC], ALU.subtract)
                last.then_inc(pooled, 1)
                mark(pooled)
                dve.wait_ge(kk_ss, l + 1)
                settle()
                v.tensor_scalar(tm[5], ps[:, 4:8, 0:T], 1e-24 / HD, None, ALU.max).then_inc(kk_floor, 1)
                mark(kk_floor)
                dve.wait_ge(root_done, 5 * l + 2)
                settle()
                link(v.reciprocal(tmp[5], tmp[5]))
                settle()
                op(v.scalar_tensor_tensor(tmp[3], tmp[3], -(HD ** -0.5), tmp[5], ALU.mult, ALU.mult))
                dve.wait_ge(lora_taken, 2 * l + 2)
                settle()
                link(v.tensor_scalar(tmp[4], tmp[4], 1.0, 0.5, ALU.add, ALU.mult))
                settle()
                for j in range(NPAIR):
                    last = op(v.tensor_scalar(tm[6][:, j, :], tm[4][:, j, :], p_(l, "ka", j), omka[:, j:j + 1], ALU.mult, ALU.add))
                dve.wait_ge(dve_step, last)
                settle()
                link(v.tensor_tensor(tm[6], tm[6], zk, ALU.mult))
                settle()
                link(v.scalar_tensor_tensor(tmp[4], tmp[3], -1.0, tmp[4], ALU.mult, ALU.mult))
                settle()
                link(v.tensor_tensor(tm[5], tm[6], zr, ALU.mult))
                settle()
                v.tensor_tensor(tm[5], tm[5], wide(p_(l, "rk"), T), ALU.mult).then_inc(bonus_in, 1)
                mark(bonus_in)
                dve.wait_ge(decay_exp, 3 * l + 3)
                settle()
                for c, (o, n) in enumerate(CHUNKS):
                    op(v.tensor_copy(chunk_decay[:, c, :], tm[1][:, :, o + n - 1]))
                settle()
                for o, n, k in SPANS:
                    for part, h in ((LOW, 0), (HIGH, 1)):
                        op(v.tensor_tensor(halves(bd_a, part, h, o, n, k), cols(tm[3], part, o, n, k), cols(tm[2], part, o, n, k), ALU.mult))
                        op(v.tensor_tensor(halves(bd_b, part, h, o, n, k), cols(tm[4], part, o, n, k), cols(tm[0], part, o, n, k), ALU.mult))
                        op(v.tensor_tensor(halves(bd_k, part, h, o, n, k), cols(tm[6], part, o, n, k), cols(tm[0], part, o, n, k), ALU.mult))
                        op(v.tensor_copy(halves(bd_v, part, h, o, n, k), cols(zv, part, o, n, k)))
                    op(v.tensor_tensor(halves(pair_ar, ALLP, 0, o, n, k), cols(tm[3], ALLP, o, n, k), cols(tm[2], ALLP, o, n, k), ALU.mult))
                    op(v.tensor_tensor(halves(pair_ar, ALLP, 1, o, n, k), cols(zr, ALLP, o, n, k), cols(tm[1], ALLP, o, n, k), ALU.mult))
                settle()
                for j in range(NPAIR):
                    dve.wait_ge(z_taken, 26 * l + 23 + j)
                    last = op(v.scalar_tensor_tensor(glu[:, j, TAPS - 1:], yB[:, j, :], 1.0, glu[:, j, TAPS - 1:], ALU.add, ALU.mult))
                conv_last = [last] * NPAIR
                dve.wait_ge(bonus_ready, l + 1)
                settle()
                v.scalar_tensor_tensor(bonus, ps[:, 4:8, 0:T], float(HD), zv, ALU.mult, ALU.mult).then_inc(wkv_in, 1)
                mark(wkv_in)

                def conv(first, count):
                    for i in range(first, min(first + count, TAPS * NPAIR)):
                        k, j = divmod(i, NPAIR)
                        w = taps[:, l * NPAIR * TAPS + j * TAPS + k:][:, 0:1]
                        dve.wait_ge(dve_step, conv_last[j])
                        if k == 0:
                            ins = v.tensor_scalar(yB[:, j, :], glu[:, j, 0:T], w, p_(l, "conv_b", j), ALU.mult, ALU.add)
                        else:
                            ins = v.scalar_tensor_tensor(yB[:, j, :], glu[:, j, k:k + T], w, yB[:, j, :], ALU.mult, ALU.add)
                        if i == TAPS * NPAIR - 1:
                            ins.then_inc(conv_done, 1)
                            mark(conv_done)
                        else:
                            conv_last[j] = op(ins)

                tap = 0
                for c, g in ORDER:
                    if taker(g) != "dve" and g != "TN":
                        continue
                    o, n = CHUNKS[c]
                    b = c % 2
                    rows = 2 * n
                    kind = kind_of(g)
                    bank = ps[0:rows, 4 * b + BANK[kind], 0:4 * rows]
                    masks = (lambda lv: [cu[0:rows, (CU_64 if n == HD else CU_16) + (2 * lv + i) * rows:][:, 0:rows]
                                         .unsqueeze(1).broadcast_to([rows, NPAIR, rows]) for i in range(2)])
                    flat = (lambda ap: ap.rearrange("p (j c) -> p j c", j=NPAIR))
                    if g == "TN":
                        taken(dve, l, c, "TN")
                        dve.wait_ge(w_id, l * NCH + c + 1)
                        if c < 2:
                            dve.wait_ge(dve_step, steps[0])
                        taken(dve, l, c, "M1")
                        settle()
                        v.copy_predicated(cb(b, S_X, rows, rows), masks(0)[0], cb(b, S_W, rows, rows))
                        settle()
                        v.copy_predicated(cb(b, S_XT, rows, rows), masks(0)[1], cb(b, S_NT, rows, rows)).then_inc(x_init, 1)
                        mark(x_init)
                    else:
                        dve.wait_ge(w_prod, wkv_count(l, c, g))
                        if g in ("M1", "M2"):
                            q = bank.rearrange("p (j h n) -> p j h n", j=NPAIR, h=2)
                            strict = c_(f"strict{n}", rows).rearrange("p (h n) -> p h n", h=2).unsqueeze(1).broadcast_to([rows, NPAIR, 2, n])
                            incl = c_(f"incl{n}", rows).unsqueeze(1).broadcast_to([rows, NPAIR, n])
                            dst = cb(b, S_W if g == "M1" else S_MAK, rows, rows).rearrange("p j (h n) -> p j h n", h=2)
                            settle()
                            v.tensor_tensor(dst, q[:, :, 0:1, :].broadcast_to([rows, NPAIR, 2, n]), strict, ALU.mult)
                            settle()
                            v.tensor_tensor(mr(b, 0 if g == "M1" else 1, rows), q[:, :, 1, :], incl, ALU.mult).then_inc(w_dve, 1)
                            mark(w_dve)
                        elif kind in "PQ":
                            if g == "P1":
                                dve.wait_ge(x_init, l * NCH + c + 1)
                            i = 0 if kind == "P" else 1
                            settle()
                            v.copy_predicated(cb(b, (S_X, S_XT)[i], rows, rows), masks(int(g[1:]))[i], flat(bank)).then_inc(w_dve, 1)
                            mark(w_dve)
                        else:
                            full = flat(ps[:, 4 * b + BANK[kind], :])
                            if c > 0:
                                taken(dve, l, c - 1, "S")
                            settle()
                            link(v.tensor_tensor(state, state, full, ALU.add))
                            settle()
                            v.tensor_tensor(state, state, wide(chunk_decay[:, c, :], P), ALU.mult).then_inc(w_dve, 1)
                            mark(w_dve)
                    conv(tap, 2)
                    tap += 2
                conv(tap, TAPS * NPAIR)

                def merge(i):
                    j = i % KD
                    dve.wait_ge(merge_ready, 24 * l + i + 1)
                    dve.wait_ge(gate_done, 24 * l + i + 1)
                    prod = ps[:, 2 * (i % 2), 0:T - c0]
                    if i < KD:
                        settle()
                        v.scalar_tensor_tensor(merged[:, j, c0:T], th2[:, i % 2, c0:T], 1.0, prod, ALU.add, ALU.mult).then_inc(merge_taken, 1)
                        mark(merge_taken)
                    else:
                        settle()
                        link(v.scalar_tensor_tensor(th2[:, i % 2, c0:T], th2[:, i % 2, c0:T], 1.0, prod, ALU.add, ALU.mult))
                        if i % KD == 0:
                            dve.wait_ge(merge_taken, 24 * l + i)
                        settle()
                        v.tensor_tensor(merged[:, j, c0:T], merged[:, j, c0:T], th2[:, i % 2, c0:T], ALU.add).then_inc(merge_taken, 1)
                        mark(merge_taken)

                taken(dve, l, NCH - 1, "Y")
                dve.wait_ge(stat_ready, 4 * l + 1)
                settle()
                v.tensor_tensor(tm[2], yA, ps[:, 4:8, 0:T], ALU.subtract).then_inc(stat_cen, 1)
                mark(stat_cen)
                dve.wait_ge(conv_done, l + 1)
                dve.wait_ge(stat_ready, 4 * l + 2)
                settle()
                v.tensor_tensor(tm[3], yB, ps[:, 4, 0:T].unsqueeze(1).broadcast_to([P, NPAIR, T]), ALU.subtract).then_inc(stat_cen, 1)
                mark(stat_cen)
                for i in range(4):
                    merge(i)
                dve.wait_ge(root_done, 5 * l + 3)
                settle()
                link(v.reciprocal(tmp[4], tmp[4]))
                settle()
                link(v.tensor_tensor(tmp[2], tmp[2], tmp[4], ALU.mult))
                settle()
                for j in range(NPAIR):
                    last = op(v.tensor_scalar(tm[2][:, j, :], tm[2][:, j, :], p_(l, "lnx_w", j), p_(l, "lnx_b", j), ALU.mult, ALU.add))
                dve.wait_ge(dve_step, last)
                settle()
                op(v.tensor_tensor(tm[2], tm[2], bonus, ALU.add))
                for i in range(4, 6):
                    merge(i)
                dve.wait_ge(root_done, 5 * l + 4)
                settle()
                link(v.reciprocal(nrm, nrm))
                settle()
                link(v.tensor_tensor(tm[3], tm[3], nrm.unsqueeze(1).broadcast_to([P, NPAIR, T]), ALU.mult))
                settle()
                for j in range(NPAIR):
                    last = v.tensor_scalar(yB[:, j, :], tm[3][:, j, :], p_(l, "b_g", j), p_(l, "b_b", j), ALU.mult, ALU.add)
                last.then_inc(yb_lin, 1)
                mark(yb_lin)
                dve.wait_ge(yb_lin, l + 1)
                dve.wait_ge(yb_tanh, l + 1)
                settle()
                link(v.scalar_tensor_tensor(yB_flat, tmp[1], 1.0, yB_flat, ALU.add, ALU.mult))
                settle()
                v.tensor_scalar(yB_flat, yB_flat, 0.5, None, ALU.mult).then_inc(yb_done, 1)
                mark(yb_done)
                for i in range(6, 8):
                    merge(i)
                dve.wait_ge(g_ready, l + 1)
                settle()
                v.tensor_tensor(yA, tm[2], ps[:, 4:8, 0:T], ALU.mult).then_inc(ya_done, 1)
                mark(ya_done)
                for i in range(8, 24):
                    merge(i)
                settle()
                for i in range(KD):
                    dve.wait_ge(out_ready, KD * l + i + 1)
                    last = v.scalar_tensor_tensor(hT[:, i, c0:T], ps[:, i, 0:T - c0], 0.5, hT[:, i, c0:T], ALU.mult, ALU.add)
                last.then_inc(h_ready, 1)
                mark(h_ready)
                dve.wait_ge(h_ready, 2 * l + 2)
                norm(2 * l + 1, "ffn_g", l, c0)
                if l == 0:
                    for ft in range(FT):
                        b4 = 4 * (ft // 2 % 2) + ft % 2
                        dve.wait_ge(hu_gate, ft + 1)
                        settle()
                        link(v.scalar_tensor_tensor(ftm[:, ft % 2, :], fth[:, ft % 4, :], 1.0, ps[:, b4, 0:T], ALU.add, ALU.mult))
                        settle()
                        v.scalar_tensor_tensor(hid[:, ft, :], ftm[:, ft % 2, :], 0.5, ps[:, b4 + 2, 0:T], ALU.mult, ALU.mult).then_inc(hu_taken, 1)
                        mark(hu_taken)
                    dve.wait_ge(down_ready, 1)
                    settle()
                    for k in range(KD):
                        last = v.tensor_tensor(hT[:, k, :], hT[:, k, :], ps[:, k, 0:T], ALU.add)
                    last.then_inc(h_ready, 1)
                    mark(h_ready)
                    dve.wait_ge(h_ready, 3)

            settle()
            for i in range(4):
                dve.wait_ge(tr_ready, 5 + i)
                v.tensor_copy(hres[:, i // 2, i % 2 * 512:(i % 2 + 1) * 512], ps[:, 4 + i, :]).then_inc(res_taken, 1)
                mark(res_taken)
            dve.wait_ge(moe_in, 48)
            dve.wait_ge(logit_ready, 1)
            both = lambda ap: ap.unsqueeze(2).broadcast_to([P, 2, E])
            settle()
            link(v.tensor_tensor(lg, ps[:, 0, 0:2 * E].rearrange("p (i e) -> p i e", i=2), rout_b[:, :].unsqueeze(1).broadcast_to([P, 2, E]), ALU.add))

            def first_max(src, m, eq, first):
                settle()
                link(v.tensor_reduce(m, src, AX_X, ALU.max))
                settle()
                link(v.tensor_tensor(eq, src, both(m), ALU.is_equal))
                settle()
                for i in range(2):
                    last = op(v.tensor_tensor_scan(cnt1[:, i, :], c_("ones")[:, 0:E], eq[:, i, :], 0.0, ALU.mult, ALU.add))
                dve.wait_ge(dve_step, last)
                settle()
                link(v.scalar_tensor_tensor(first, cnt1, 1.0, eq, ALU.is_equal, ALU.mult))

            first_max(lg, mx[:, :, 0], eq1, first1)
            settle()
            link(v.scalar_tensor_tensor(lg2, first1, -1e30, lg, ALU.mult, ALU.add))
            first_max(lg2, mx[:, :, 1], eq2, first2)
            settle()
            v.tensor_tensor(mx[:, :, 2], mx[:, :, 1], mx[:, :, 0], ALU.subtract).then_inc(gap_ready, 1)
            mark(gap_ready)
            settle()
            v.tensor_tensor(sel, first1, first2, ALU.add).then_inc(sel_ready, 1)
            mark(sel_ready)
            dve.wait_ge(gap_exp, 1)
            settle()
            link(v.tensor_scalar(mx[:, :, 4], mx[:, :, 3], 1.0, None, ALU.add))
            settle()
            link(v.reciprocal(mx[:, :, 4], mx[:, :, 4]))
            settle()
            link(v.tensor_tensor(mx[:, :, 5], mx[:, :, 4], mx[:, :, 3], ALU.mult))
            settle()
            link(v.tensor_tensor(gw, first1, both(mx[:, :, 4]), ALU.mult))
            settle()
            link(v.tensor_tensor(lg2, first2, both(mx[:, :, 5]), ALU.mult))
            settle()
            op(v.tensor_tensor(gw, gw, lg2, ALU.add))
            dve.wait_ge(pos_ready, 1)
            dve.wait_ge(sel_ready, 1)
            settle()
            link(v.scalar_tensor_tensor(pos0, ps[:, 1, 0:2 * E].rearrange("p (i e) -> p i e", i=2), 1.0, sel, ALU.add, ALU.mult))
            settle()
            link(v.tensor_scalar(pos0, pos0, -1.0, None, ALU.add))
            settle()
            op(v.tensor_scalar(pos1, pos0, -float(SLOTS), None, ALU.add))
            settle()
            v.tensor_copy(count_i.bitcast(I32), ps[:, 1, 2 * E:3 * E]).then_inc(route_done, 1)
            mark(route_done)
            dve.wait_ge(dve_step, steps[0])
            dve.wait_ge(route_done, 1)
            dve.wait_ge(tr_taken, 4)
            dve.wait_ge(res_taken, 4)

            def expert_pass(e, n, pos):
                for tt in range(2):
                    v.tensor_scalar(pick[:, tt, :], c_("slot"), pos[:, tt, bass.ds(e, 1)], None, ALU.is_equal)
                for tt in range(2):
                    last = v.tensor_scalar(pickw[:, tt, :], c_("slot"), pos[:, tt, bass.ds(e, 1)], gw[:, tt, bass.ds(e, 1)], ALU.is_equal, ALU.mult)
                last.then_inc(pick_ready, 1)

                def w_rest(i):
                    hi, lo = wsplit[i % SPLITS]
                    dve.wait_ge(w_hi, n * FFN_UNITS + i + 1)
                    v.tensor_tensor(lo, eslots[i % ERING], hi.bitcast(F32), ALU.subtract).then_inc(ring_used, 1)

                w_rest(0)
                for h in range(2):
                    dve.wait_ge(gather_taken, n * 3 + 2 + h)
                    c = slice(h * 512, (h + 1) * 512)
                    v.tensor_tensor(xe_s[1][:, c], ps[:, 4 + h, :], xe_s[0][:, c].bitcast(F32), ALU.subtract).then_inc(xe_lo_done, 1)
                for i in range(1, FFN_UNITS):
                    g, d = (i - 4) // 4, (i - 4 * FG) // 2
                    if i % 4 == 0 and g < FG:
                        dve.wait_ge(egate_tanh, n * FG + g + 1)
                        v.scalar_tensor_tensor(etm[:, g % 2, :], eth[:, g % 2, :], 1.0, ps[:, g % 2, 0:256], ALU.add, ALU.mult).then_inc(moe_step, 1)
                    if i % 4 == 2 and i >= 4 and g < FG:
                        dve.wait_ge(moe_step, n * FG + g + 1)
                        dve.wait_ge(split_used, n * FFN_UNITS + SPLITS + 4 * g + 4)
                        v.scalar_tensor_tensor(hid_t[:, g * 256:(g + 1) * 256], etm[:, g % 2, :], 0.5, ps[:, 4 + g % 2, 0:256],
                                               ALU.mult, ALU.mult).then_inc(ehid_done, 1)
                    w_rest(i)
                    if d >= 0 and i % 2 == 0:
                        dve.wait_ge(ehid_hi, n * FG + d + 1)
                        v.tensor_tensor(hid_s[d % 2][1], ps[:, 2 + d % 2, 0:256], hid_s[d % 2][0].bitcast(F32), ALU.subtract).then_inc(ehid_lo, 1)
                for h in range(2):
                    for tt in range(2):
                        dve.wait_ge(scat_ready, n * 4 + 2 * h + tt + 1)
                        part = hres[:, tt, h * 512:(h + 1) * 512]
                        v.tensor_tensor(part, part, ps[:, YBANK[tt, h], :], ALU.add).then_inc(scat_taken, 1)
                dve.wait_ge(scat_taken, n * 4 + 4)

            with dve.Fori(0, E) as e:
                expert_pass(e, e, pos0)
            with dve.register("passes") as passes:
                dve.reg_mov(passes, E)
                for q in range(1, PASSES):
                    with dve.Fori(0, E) as e:
                        count = dve.value_load(count_i[0:1, bass.ds(e, 1)].bitcast(I32))
                        with dve.If(count > q * SLOTS):
                            expert_pass(e, dve.snap(passes), pos1)
                            dve.reg_add(passes, passes, 1)
            for i in range(2):
                dve.wait_ge(root_done, 5 * DEPTH + 1 + i)
                link(v.reciprocal(ssq[:, i:i + 1], ssq[:, i:i + 1]))
                v.scalar_tensor_tensor(ntok[:, i, :], hres[:, i, :], ssq[:, i:i + 1], fg, ALU.mult, ALU.mult).then_inc(fin_done, 1)


def kernel(**inputs):
    import concourse.bacc as bacc
    from concourse.bass_utils import run_bass_kernel_spmd

    a = {k: np.asarray(v) for k, v in inputs.items()}

    def channels(v):
        return np.transpose(v.reshape(DEPTH, -1, P), (0, 2, 1))

    names = dict(gate_b="gate_b", w0="a_w0", a0="a_a0", mix_g="mix_norm_g", mu="a_mu", kk="a_kk", ka="a_ka", rk="a_rk",
                 lnx_w="a_lnx_w", lnx_b="a_lnx_b", conv_b="b_conv_b", b_g="b_ln_g", b_b="b_ln_b", c_scale="c_scale", ffn_g="ffn_norm_g")
    const_f, const_u = constants()
    arrays = dict(
        x=a["x"], meta=a["meta_tokens"], w_in=a["w_in"],
        lora=np.concatenate([a["a_w2"], a["a_a2"]], 1), g2=a["a_g2"], pool_w=a["c_pool_w"],
        params=np.concatenate([channels(a[names[k]]) for k in COLS], 2),
        conv_w=np.ascontiguousarray(np.transpose(a["b_conv_w"].reshape(DEPTH, TAPS, NPAIR, P), (0, 3, 2, 1))).reshape(DEPTH, P, NPAIR * TAPS),
        proj_a=a["proj_a"], proj_b=a["proj_b"], proj_c=a["proj_c"], w_out=a["w_out"],
        ffn_gate=a["ffn_gate"], ffn_up=a["ffn_up"], ffn_down=a["ffn_down"], router_w=a["router_w"], router_b=a["router_b"],
        exp_gate=a["exp_gate"], exp_up=a["exp_up"], exp_down=a["exp_down"], final_g=a["final_norm_g"],
        const_f=const_f, const_u=const_u)
    nc = bacc.Bacc("TRN2", target_bir_lowering=False, num_devices=1)
    given, args = {}, []
    for name, v in arrays.items():
        given[f"in_{name}"] = np.ascontiguousarray(v)
        args.append(nc.dram_tensor(f"in_{name}", v.shape, mybir.dt.from_np(v.dtype), kind="ExternalInput").ap())
    args.append(nc.dram_tensor("out_0", (1, SEQ, D), F32, kind="ExternalOutput").ap())
    build(nc, *args)
    r = run_bass_kernel_spmd(nc, [given], core_ids=[0])
    return r.results[0]["out_0"]
```

```python
from contextlib import ExitStack

import numpy as np

import concourse.bass as bass
from concourse import mybir

F32 = mybir.dt.float32
F32R = mybir.dt.float32r
U8 = mybir.dt.uint8
I32 = mybir.dt.int32
ALU = mybir.AluOpType
ACT = mybir.ActivationFunctionType
AX_X = mybir.AxisListType.X

P = 128
D = 1024
KD = D // P
SEQ = 256
META = 16
T = META + SEQ
DEPTH = 2
HD = 64
NPAIR = 4
AW = NPAIR * P
A_TILES, C_TILES, B_TILES = 14, 4, 8
A_IN = A_TILES * P
TAPS = 31
PADC = 16
F = 2816
FT = F // P
E = 8
SLOTS = 128
PASSES = SEQ // SLOTS
FG = F // 256
CONV_DVE = 3
CONV_POOL = (2 * TAPS - 1) * (NPAIR - CONV_DVE)
SPLITS = 3
CHUNKS = [(0, META)] + [(META + i * HD, HD) for i in range(SEQ // HD)]
NCH = len(CHUNKS)
RMS_EPS, LN_EPS, LNX_EPS = 1e-6, 1e-5, 64e-5
DECAY = float(np.exp(-0.5))

COLS = dict(gate_b=(0, 24), w0=(24, 4), a0=(28, 4), mix_g=(32, 8), mu=(40, 14), kk=(54, 4), ka=(58, 4), rk=(62, 4),
            lnx_w=(66, 4), lnx_b=(70, 4), conv_b=(74, 4), b_g=(78, 4), b_b=(82, 4), c_scale=(86, 4), ffn_g=(90, 8))
NPAR = 98

CF = dict(ident=(0, 128), head_mean=(128, 128), d_mean=(256, 128), c_mean=(384, 128), strict64=(512, 128),
          incl64=(640, 64), strict16=(704, 32), incl16=(736, 16), inv_win=(752, 64), before=(816, 128),
          ones=(944, 128), slot=(1072, 128), eps=(1200, 3))
NCF = 1203
CU_SCAN = 0
CU_64 = T * NPAIR
CU_16 = CU_64 + 6 * 2 * 128
NCU = CU_16 + 4 * 2 * 32
ARENA = 30912

RING = 7
ERING = 22
EARLY = 8
UNIT = 1024
Z_ORDER = [12, 13, 4, 5, 6, 7, 0, 1, 2, 3, 8, 9, 10, 11] + [22, 23, 24, 25] + list(range(14, 22))
W_IN_UNITS = 26
MIX_UNITS = W_IN_UNITS + 3 * 4 * 3 + 8
FFN_UNITS = 11 * 4 + FT
MOE_UNIT0 = 2 * MIX_UNITS + FFN_UNITS
RAW = {l * (MIX_UNITS + FFN_UNITS) + W_IN_UNITS + 3 * i for l in range(DEPTH) for i in range(12)}
KIND_AT = [sum(w in RAW for w in range(u)) for u in range(MOE_UNIT0)]
E_SPLIT0 = MOE_UNIT0 - len(RAW)


def split_at(u):
    return u - KIND_AT[u]




def constants():
    f = np.zeros((P, NCF), np.float32)
    u = np.zeros((P, NCU), np.float32)

    def put(name, a):
        f[:a.shape[0], CF[name][0]:CF[name][0] + a.shape[1]] = a

    i = np.arange(P)
    put("ident", np.eye(P))
    put("head_mean", (i[:, None] // HD == i[None] // HD) / HD)
    put("d_mean", np.full((P, P), 1 / D))
    put("c_mean", np.full((P, P), 1 / AW))
    for n in (64, 16):
        r = np.arange(2 * n)
        same = r[:, None] // n == r[None] // n
        put(f"strict{n}", same & (r[:, None] < r[None]))
        put(f"incl{n}", r[:, None] % n <= np.arange(n)[None])
        for lv in range(6 if n == 64 else 4):
            b = 1 << lv
            s, t = r[:, None] % n, r[None] % n
            m = same & (s // (2 * b) == t // (2 * b)) & (s // b % 2 == 0) & (t // b % 2 == 1)
            at = (CU_64 if n == 64 else CU_16) + lv * 2 * 2 * n
            u[:2 * n, at:at + 2 * n] = m
            u[:2 * n, at + 2 * n:at + 4 * n] = m.T
    put("inv_win", np.tile(np.concatenate([1.0 / np.minimum(np.arange(1, 17), 2 << j) for j in range(4)])[None], (P, 1)))
    put("before", i[:, None] < i[None])
    put("ones", np.ones((P, P)))
    put("slot", np.tile(i[None], (P, 1)))
    put("eps", np.tile(np.array([RMS_EPS, LN_EPS, LNX_EPS])[None], (P, 1)))
    starts = np.ones(T)
    starts[[o for o, _ in CHUNKS]] = 0
    u[:, CU_SCAN:CU_SCAN + NPAIR * T] = np.tile(starts, NPAIR)[None]
    return f, u


def build(nc, x, meta, w_in, lora, g2, pool_w, params, conv_w, proj_a, proj_b, proj_c, w_out,
          ffn_gate, ffn_up, ffn_down, router_w, router_b, exp_gate, exp_up, exp_down, final_g, const_f, const_u, out):
    ctx = ExitStack()
    with ctx:
        def sb(name, cols, dt=F32):
            return ctx.enter_context(nc.sbuf_tensor(name, [P, cols], dt))

        def sem(name):
            return ctx.enter_context(nc.semaphore(name))

        ps = ctx.enter_context(nc.psum_tensor("ps", [P, 8, 512], F32))

        ring = sb("ring", RING * UNIT)
        cf = sb("cf", NCF)
        cu = sb("cu", NCU, U8)
        par = sb("par", DEPTH * NPAR)
        half = sb("half", 32)
        half_b = sb("half_b", 8)
        omka = sb("omka", NPAIR)
        taps = sb("taps", DEPTH * NPAIR * TAPS)
        lora_w = sb("lora_w", AW)
        g2_w = sb("g2_w", AW)
        pool_wt = sb("pool_wt", AW)
        rout_w = sb("rout_w", KD * E)
        rout_b = sb("rout_b", E)
        arena = sb("arena", ARENA)
        split = sb("split", SPLITS * 2 * UNIT + 2 * KD * T, F32R)
        at = [0]

        def take(n):
            v = arena[:, at[0]:at[0] + n]
            at[0] += n
            return v

        hT = take(KD * T).rearrange("p (k t) -> p k t", k=KD)
        mixer_at = at[0]
        za = take(A_TILES * (T + 1)).rearrange("p (j t) -> p j t", j=A_TILES)
        zr, zk, zv = (za[:, 4 * i:4 * i + 4, 1:T + 1] for i in range(3))
        yA, bonus = zr, zk
        chunk_at = at[0]
        region = take(2 * 4608)
        tmp = [region[:, i * NPAIR * T:(i + 1) * NPAIR * T] for i in range(7)]
        tm = [t.rearrange("p (j t) -> p j t", j=NPAIR) for t in tmp]
        merged = region[:, 5 * NPAIR * T:7 * NPAIR * T].rearrange("p (k t) -> p k t", k=KD)
        xt = region[:, 0:3 * D].rearrange("p (i d) -> p i d", i=3)
        stage = arena[:, at[0]:at[0] + NCU]
        bd_a, bd_b, bd_k, bd_v, pair_ar = (take(2 * NPAIR * T) for _ in range(5))
        sq = pair_ar.rearrange("p (k t) -> p k t", k=KD)
        nT = sq
        mix_v = pair_ar[:, 0:NPAIR * T].rearrange("p (j t) -> p j t", j=NPAIR)
        pool1 = region[:, 0:4 * (T + PADC)].rearrange("p (j t) -> p j t", j=4)
        pool2 = region[:, 4 * (T + PADC):7 * (T + PADC)].rearrange("p (j t) -> p j t", j=3)
        zc = take(NPAIR * (T + PADC)).rearrange("p (j t) -> p j t", j=NPAIR)
        glu = take(NPAIR * (T + TAPS - 1)).rearrange("p (j t) -> p j t", j=NPAIR)
        yB_flat = take(NPAIR * T)
        yB = yB_flat.rearrange("p (j t) -> p j t", j=NPAIR)
        yC = zc[:, :, PADC:]
        th2 = take(2 * T).rearrange("p (j t) -> p j t", j=2)
        state = take(NPAIR * P).rearrange("p (j v) -> p j v", j=NPAIR)
        chunk_decay = take(NCH * NPAIR).rearrange("p (c j) -> p c j", c=NCH)
        nrm = take(T)
        mixer_end = at[0]

        def cb(b, slot, w, rows, n=1):
            o = b * 4608 + slot * 512
            return region[0:rows, o:o + 4 * w].rearrange("p (j c) -> p j c", j=NPAIR)

        at[0] = mixer_at
        hid_flat = take(FT * T)
        hid = hid_flat.rearrange("p (f t) -> p f t", f=FT)
        fth = take(4 * T).rearrange("p (r t) -> p r t", r=4)
        ftm = take(2 * T).rearrange("p (r t) -> p r t", r=2)
        assert at[0] <= mixer_end

        bd_at = chunk_at + 2 * 4608
        tail_at = bd_at + 5 * 2 * NPAIR * T
        bd_slots = [arena[:, bd_at + i * UNIT:bd_at + (i + 1) * UNIT] for i in range((tail_at - bd_at) // UNIT)]
        eslots = bd_slots[:EARLY]
        eslots += [ring[:, u % RING * UNIT:(u % RING + 1) * UNIT] for u in range(MOE_UNIT0, MOE_UNIT0 + RING)]
        eslots += bd_slots[EARLY:]
        for i in range(KD * T // UNIT):
            eslots.append(arena[:, i * UNIT:(i + 1) * UNIT])
        for i in range((mixer_end - tail_at) // UNIT):
            eslots.append(arena[:, tail_at + i * UNIT:tail_at + (i + 1) * UNIT])
        assert EARLY * UNIT <= 4 * 2 * NPAIR * T and len(eslots) >= ERING, len(eslots)
        at[0] = mixer_at
        hid_t = take(F)
        eth = take(2 * 256).rearrange("p (r c) -> p r c", r=2)
        etm = take(2 * 256).rearrange("p (r c) -> p r c", r=2)
        ntok = take(2 * D).rearrange("p (i d) -> p i d", i=2)
        hres = take(2 * D).rearrange("p (i d) -> p i d", i=2)
        ye = take(D)
        pick = take(2 * SLOTS).rearrange("p (i s) -> p i s", i=2)
        pickw = take(2 * SLOTS).rearrange("p (i s) -> p i s", i=2)
        pickT = take(2 * P)
        lg, eq1, eq2, first1, first2, cnt1, lg2, sel, pos1 = (
            take(2 * E).rearrange("p (i e) -> p i e", i=2) for _ in range(9))
        pos0x, gwx = (take(2 * (E + 1)).rearrange("p (i e) -> p i e", i=2) for _ in range(2))
        pos0, gw = pos0x[:, :, 0:E], gwx[:, :, 0:E]
        mx = take(2 * 6).rearrange("p (i c) -> p i c", c=6)
        count_i = take(E)
        fg = take(D)
        ssq = take(4)
        assert at[0] <= bd_at, (at[0], bd_at)
        if len(eslots) < ERING:
            eslots.append(arena[:, at[0]:at[0] + UNIT])

        def parts(o, n, buffers):
            return [[split[:, o + (2 * b + i) * n:o + (2 * b + i + 1) * n] for i in range(2)] for b in range(buffers)]

        wsplit = parts(0, UNIT, SPLITS)
        xr_at = SPLITS * 2 * UNIT
        xr_flat = parts(xr_at, KD * T, 1)[0]
        xr = [v.rearrange("p (k t) -> p k t", k=KD) for v in xr_flat]
        hid_r = parts(xr_at, T, 4)
        xe_s = parts(xr_at, KD * SLOTS, 1)[0]
        hid_s = parts(xr_at + 2 * KD * SLOTS, 256, 2)
        YBANK = {(0, 0): 0, (1, 0): 1, (0, 1): 2, (1, 1): 3}

        def c_(name, rows=P):
            return cf[0:rows, CF[name][0]:CF[name][0] + CF[name][1]]

        def p_(l, name, j=None):
            o, w = COLS[name]
            o += l * NPAR
            return par[:, o:o + w] if j is None else par[:, o + j:o + j + 1]

        def wide(ap, n):
            return ap.unsqueeze(2).broadcast_to([ap.shape[0], ap.shape[1], n])

        def block(buf, rows, j, o, n):
            return buf[0:rows, j * 2 * T + 2 * o:j * 2 * T + 2 * o + 2 * n]

        def halves(buf, part, h, o, n, chunks):
            v = buf[part, :].rearrange("p (j c) -> p j c", j=NPAIR)[:, :, 2 * o:2 * o + 2 * n * chunks]
            return v.rearrange("p j (c h n) -> p j c h n", h=2, n=n)[:, :, :, h]

        def cols(v, part, o, n, chunks):
            return v[part, :, o:o + n * chunks].rearrange("p j (c n) -> p j c n", n=n)

        ALLP, LOW, HIGH = slice(0, P), slice(0, HD), slice(HD, P)
        SPANS = [(0, META, 1), (META, HD, NCH - 1)]

        ident_in = sem("ident_in")
        table_in = sem("table_in")
        const_in = sem("const_in")
        masks_in = sem("masks_in")
        x_in = sem("x_in")
        small_in = sem("small_in")
        moe_in = sem("moe_in")
        gain_in = sem("gain_in")
        lg_taken = sem("lg_taken")
        ring_in = [sem(f"ring_in{i}") for i in range(RING)]
        raw_used = sem("raw_used")
        w_lo = sem("w_lo")
        e_split = sem("e_split")
        n_f32 = sem("n_f32")
        m_hi, m_lo = sem("m_hi"), sem("m_lo")
        hid_hi, hid_lo = sem("hid_hi"), sem("hid_lo")
        prep_done = sem("prep_done")
        blocks_zero = sem("blocks_zero")
        masks_done = sem("masks_done")
        half_done = sem("half_done")
        dve_step = sem("dve_step")
        act_step = sem("act_step")
        xt_ready, xt_taken = sem("xt_ready"), sem("xt_taken")
        h_ready = sem("h_ready")
        sq_done, ssq_ready, n_ready = sem("sq_done"), sem("ssq_ready"), sem("n_ready")
        z_ready, z_taken = sem("z_ready"), sem("z_taken")
        lora_mixed, lora_act = sem("lora_mixed"), sem("lora_act")
        lora_ready, lora_taken = sem("lora_ready"), sem("lora_taken")
        gd_tanh, gd_done = sem("gd_tanh"), sem("gd_done")
        glu_done = sem("glu_done")
        kk_sq, kk_ss = sem("kk_sq"), sem("kk_ss")
        decay_log, decay_exp = sem("decay_log"), sem("decay_exp")
        bonus_in, bonus_ready = sem("bonus_in"), sem("bonus_ready")
        wkv_in = sem("wkv_in")
        pooled, pool_ready, pool_taken = sem("pooled"), sem("pool_ready"), sem("pool_taken")
        merge_ready, gate_done, merge_taken = sem("merge_ready"), sem("gate_done"), sem("merge_taken")
        out_ready = sem("out_ready")
        w_prod, w_dve, w_act = sem("w_prod"), sem("w_dve"), sem("w_act")
        x_init = sem("x_init")
        w_id = sem("w_id")
        conv_done = sem("conv_done")
        conv_pool = sem("conv_pool")
        stat_ready = sem("stat_ready")
        stat_cen, stat_sq = sem("stat_cen"), sem("stat_sq")
        kk_floor = sem("kk_floor")
        root_done = sem("root_done")
        yb_lin, yb_tanh = sem("yb_lin"), sem("yb_tanh")
        yb_done, ya_done = sem("yb_done"), sem("ya_done")
        g_ready = sem("g_ready")
        hu_ready, hu_gate, hu_taken = sem("hu_ready"), sem("hu_gate"), sem("hu_taken")
        down_ready, down_taken = sem("down_ready"), sem("down_taken")
        tr_ready, tr_taken = sem("tr_ready"), sem("tr_taken")
        logit_ready, gap_ready, gap_exp = sem("logit_ready"), sem("gap_ready"), sem("gap_exp")
        sel_ready, pos_ready, route_done = sem("sel_ready"), sem("pos_ready"), sem("route_done")
        pick_ready, gather_ready, gather_taken = sem("pick_ready"), sem("gather_ready"), sem("gather_taken")
        moe_step = sem("moe_step")
        ering_in = [sem(f"ering_in{i}") for i in range(ERING)]
        w_hi = sem("w_hi")
        split_used = sem("split_used")
        egate_tanh, ehid_done = sem("egate_tanh"), sem("ehid_done")
        ehid_tr, ehid_hi, ehid_lo = sem("ehid_tr"), sem("ehid_hi"), sem("ehid_lo")
        xe_lo_done = sem("xe_lo_done")
        y_ready, y_taken = sem("y_ready"), sem("y_taken")
        scat_ready, scat_taken = sem("scat_ready"), sem("scat_taken")
        fin_sq, fin_done, out_sent = sem("fin_sq"), sem("fin_done"), sem("out_sent")

        CONST_DMAS = 2

        def ss_bank(m):
            return 7 if m == 0 else 0


        def c0_of(l):
            return 0 if l < DEPTH - 1 else META

        def levels(n):
            return 5 if n == HD else 3

        START_GAP = 3

        def wkv_schedule():
            steps_of, start = {}, {}
            for c in range(NCH):
                lv_n = levels(CHUNKS[c][1])
                seq = ["M1", "M2", "TB", "TK", "TV", "TN"]
                for lv in range(1, lv_n + 1):
                    seq += [f"W{lv}", f"P{lv}"] + [f"Q{lv}"] * (lv < lv_n)
                steps_of[c] = seq + ["R", "U", "Y", "S"]
                start[c] = start[c - 2] + len(steps_of[c - 2]) if c >= 2 else START_GAP * c
            when = [(start[c] + i, c, g) for c in range(NCH) for i, g in enumerate(steps_of[c])]
            return [(c, g) for _, c, g in sorted(when, key=lambda k: k[:2])]

        ORDER = wkv_schedule()
        prod_at = {key: i + 1 for i, key in enumerate(ORDER)}

        def taker(g):
            return "act" if g in ("TB", "TK", "TV", "TN", "R", "U", "Y") or g[0] == "W" else "dve"

        act_at, dve_at = {}, {}
        for key in ORDER:
            d = act_at if taker(key[1]) == "act" else dve_at
            d[key] = len(d) + 1

        def wkv_count(l, c, g):
            return l * len(ORDER) + prod_at[(c, g)]

        def taken(eng, l, c, g):
            if taker(g) == "act":
                eng.wait_ge(w_act, l * len(act_at) + act_at[(c, g)])
            else:
                eng.wait_ge(w_dve, l * len(dve_at) + dve_at[(c, g)])

        BANK = {"M1": 0, "M2": 1, "TB": 2, "TK": 3, "TV": 0, "TN": 1, "W": 2, "P": 3, "Q": 0, "R": 1, "U": 2, "Y": 3, "S": 0}

        def kind_of(g):
            return g[0] if g[0] in "WPQ" else g

        def before_in_bank(c, g):
            seq = [k for k in ORDER if k[0] % 2 == c % 2]
            for k in reversed(seq[:seq.index((c, g))]):
                if BANK[kind_of(k[1])] == BANK[kind_of(g)]:
                    return k
            return None

        def mr(b, which, rows):
            at_ = b * 4608 + S_MR * 512 + which * 256
            return region[0:rows, at_:at_ + 2 * rows].rearrange("p (j c) -> p j c", j=NPAIR)

        S_W, S_NT, S_X, S_XT, S_MAK, S_MR, S_V, S_B, S_K = range(9)


        blk = ctx.enter_context(nc.Block())

        @blk.sync
        def _(sp):
            def slot(u):
                return ring[:, (u % RING) * UNIT:(u % RING + 1) * UNIT]

            def unit(u, shape, src):
                if u == 1:
                    sp.wait_ge(x_in, 48)
                if u >= RING:
                    before = u - RING
                    if before in RAW:
                        sp.wait_ge(raw_used, KIND_AT[before] + 1)
                    else:
                        sp.wait_ge(w_lo, split_at(before) + 1)
                dst = slot(u) if shape is None else slot(u).rearrange("p (k c) -> p k c", k=shape)
                sp.dma_start(dst, src).then_inc(ring_in[u % RING], 16)

            def columns(u, w, c):
                v = w.rearrange("(k p) c -> p k c", p=P)
                for h in range(2):
                    unit(u + h, 4, v[:, 4 * h:4 * h + 4, c:c + 256])

            def swiglu_units(u, wg, wu, wd):
                for g in range(FT // 2):
                    columns(u, wg, 256 * g)
                    columns(u + 2, wu, 256 * g)
                    u += 4
                for ft in range(FT):
                    unit(u, None, wd[ft * P:(ft + 1) * P, :])
                    u += 1

            u = 0
            for l in range(DEPTH):
                for j in Z_ORDER[::2]:
                    columns(u, w_in[l], j * P)
                    u += 2
                for b, pr in ((2, proj_c), (1, proj_b), (0, proj_a)):
                    for i in range(4):
                        unit(u, 4, pr[l].rearrange("(k p) c -> p k c", p=P)[:, :, 256 * i:256 * i + 256])
                        columns(u + 1, w_in[l], (A_TILES + B_TILES + C_TILES + KD * b) * P + 256 * i)
                        u += 3
                for i in range(4):
                    columns(u, w_out[l], 256 * i)
                    u += 2
                if l == 0:
                    swiglu_units(u, ffn_gate[0], ffn_up[0], ffn_down[0])
                    u += FFN_UNITS
            assert u == MOE_UNIT0
            wg, wu, wd = (w.rearrange("a e r c -> (a e) r c") for w in (exp_gate, exp_up, exp_down))

            def expert_units(e, n):
                g_, u_, d_ = (w[bass.ds(e, 1)].rearrange("a r c -> (a r) c") for w in (wg, wu, wd))
                gv, uv = (w.rearrange("(k p) c -> p k c", p=P) for w in (g_, u_))
                for i in range(FFN_UNITS):
                    if not isinstance(n, int) or i >= ERING:
                        sp.wait_ge(e_split, i - ERING + 1 + n * FFN_UNITS)
                    elif i < EARLY:
                        sp.wait_ge(w_prod, DEPTH * len(ORDER))
                    elif i < EARLY + RING:
                        sp.wait_ge(w_lo, E_SPLIT0 - RING + (i - EARLY) + 1)
                    else:
                        sp.wait_ge(tr_ready, 8)
                        sp.wait_ge(logit_ready, 1)
                    dst = eslots[i % ERING]
                    if i < 4 * FG:
                        g, r_ = divmod(i, 4)
                        v, h = ((gv, uv)[r_ // 2], r_ % 2)
                        sp.dma_start(dst.rearrange("p (k c) -> p k c", k=4), v[:, 4 * h:4 * h + 4, 256 * g:256 * g + 256]).then_inc(ering_in[i % ERING], 16)
                    else:
                        ft = i - 4 * FG
                        sp.dma_start(dst, d_[ft * P:(ft + 1) * P, :]).then_inc(ering_in[i % ERING], 16)

            expert_units(0, 0)
            with sp.Fori(1, E) as e:
                expert_units(e, e)
            sp.wait_ge(route_done, 1)
            with sp.register("passes") as passes:
                sp.reg_mov(passes, E)
                for q in range(1, PASSES):
                    with sp.Fori(0, E) as e:
                        count = sp.value_load(count_i[0:1, bass.ds(e, 1)].bitcast(I32))
                        with sp.If(count > q * SLOTS):
                            expert_units(e, sp.snap(passes))
                            sp.reg_add(passes, passes, 1)
            sp.wait_ge(fin_done, 2)
            for i in range(2):
                sp.dma_start(out[0, i * P:(i + 1) * P, :], ntok[:, i, :]).then_inc(out_sent, 16)
            sp.wait_ge(out_sent, 32)

        @blk.gpsimd
        def _(pool):
            pool.memset(za[:, :, 0:1], 0.0)
            pool.memset(zc[:, :, 0:PADC], 0.0)
            pool.memset(glu[:, :, 0:TAPS - 1], 0.0).then_inc(prep_done, 1)

            def small(l):
                pool.dma_start(lora_w[:, :], lora[l]).then_inc(small_in, 16)
                pool.dma_start(g2_w[:, :], g2[l]).then_inc(small_in, 16)
                pool.dma_start(pool_wt[:, :].rearrange("p (j d) -> p j d", j=NPAIR),
                               pool_w[l].rearrange("j c d -> c j d")).then_inc(small_in, 16)
            small(0)
            pool.dma_start(rout_w[:, :].rearrange("p (k e) -> p k e", e=E),
                           router_w[0].rearrange("(k p) e -> p k e", p=P)).then_inc(moe_in, 16)
            pool.dma_start(rout_b[:, :], router_b[0].partition_broadcast(P)).then_inc(moe_in, 16)

            def w_rest(first, last):
                for u in range(first, last):
                    if u in RAW:
                        continue
                    hi, lo = wsplit[split_at(u) % SPLITS]
                    pool.wait_ge(w_hi, split_at(u) + 1)
                    pool.tensor_tensor(lo, ring[:, (u % RING) * UNIT:(u % RING + 1) * UNIT], hi.bitcast(F32), ALU.subtract).then_inc(w_lo, 1)

            u = 0
            for l in range(DEPTH):
                if l > 0:
                    pool.wait_ge(h_ready, KD * (2 * l + 1))
                    pool.memset(za[:, :, 0:1], 0.0)
                    pool.memset(zc[:, :, 0:PADC], 0.0)
                    pool.memset(glu[:, :, 0:TAPS - 1], 0.0).then_inc(prep_done, 1)
                    small(l)
                w_rest(u, u + 8)
                if l == 0:
                    pool.wait_ge(masks_done, 1)
                for i, v in enumerate((bd_a, bd_b, bd_k, bd_v)):
                    w_rest(u + 8 + 2 * i, u + 10 + 2 * i)
                    pool.memset(v, 0.0)
                pool.memset(state, 0.0).then_inc(blocks_zero, 1)
                w_rest(u + 16, u + W_IN_UNITS)
                done = l * CONV_POOL
                for c in range(NCH):
                    if c >= 2:
                        for k in range((c - 2) * TAPS // 3, (c - 1) * TAPS // 3):
                            for add in (False, True):
                                for j in range(CONV_DVE, NPAIR):
                                    w = taps[:, l * NPAIR * TAPS + j * TAPS + k:][:, 0:1]
                                    if done >= NPAIR - CONV_DVE:
                                        pool.wait_ge(conv_pool, done - (NPAIR - CONV_DVE) + 1)
                                    if k == 0 and not add:
                                        ins = pool.tensor_scalar(yB[:, j, :], glu[:, j, 0:T], w, p_(l, "conv_b", j), ALU.mult, ALU.add)
                                    elif not add:
                                        ins = pool.tensor_scalar(th2[:, j - CONV_DVE, :], glu[:, j, k:k + T], w, None, ALU.mult)
                                    elif k > 0:
                                        ins = pool.tensor_tensor(yB[:, j, :], yB[:, j, :], th2[:, j - CONV_DVE, :], ALU.add)
                                    else:
                                        continue
                                    ins.then_inc(conv_pool, 1)
                                    done += 1
                    n = CHUNKS[c][1]
                    if c < 2:
                        pool.wait_ge(wkv_in, l + 1)
                    else:
                        pool.wait_ge(w_prod, wkv_count(l, c - 2, "S"))
                    eye = c_("ident", 2 * n)[:, 0:2 * n].unsqueeze(1).broadcast_to([2 * n, NPAIR, 2 * n])
                    pool.tensor_copy(cb(c % 2, 2, 2 * n, 2 * n), eye)
                    pool.tensor_copy(cb(c % 2, 3, 2 * n, 2 * n), eye).then_inc(w_id, 1)
                w_rest(u + W_IN_UNITS, u + MIX_UNITS)
                u += MIX_UNITS
                if l == 0:
                    w_rest(u, u + FFN_UNITS)
                    u += FFN_UNITS
            pool.wait_ge(h_ready, KD * 2 * DEPTH)
            pool.dma_start(fg, final_g.partition_broadcast(P)).then_inc(gain_in, 16)

        @blk.tensor
        def _(pe):
            mm = nc.tensor.matmul
            ident = c_("ident")
            release = [None]

            def open_unit(u):
                if u in RAW:
                    pe.wait_ge(ring_in[u % RING], 16 * (u // RING + 1))
                else:
                    pe.wait_ge(w_lo, split_at(u) + 1)
                if u > 0:
                    release[0] = raw_used if u - 1 in RAW else split_used
                return ring[:, (u % RING) * UNIT:(u % RING + 1) * UNIT] if u in RAW else wsplit[split_at(u) % SPLITS]

            def mmu(*a, **k):
                ins = mm(*a, **k)
                if release[0] is not None:
                    ins.then_inc(release[0], 1)
                release[0] = None
                return ins

            def mm3(o, w, x, start, stop):
                mmu(o, w[0], x[0], start=start, stop=False)
                mm(o, w[0], x[1], start=False, stop=False)
                return mm(o, w[1], x[0], start=False, stop=stop)

            def tokens(c0):
                return lambda k: [v[:, k, c0:T] for v in xr]

            def column_pair(u, outs, rhs, ready=None):
                for h in range(2):
                    w = open_unit(u + h)
                    for i, o in enumerate(outs):
                        for k in range(4):
                            if ready is not None and i == 0:
                                ready(4 * h + k)
                            at_ = k * 256 + i * P
                            last = mm3(o, [v[:, at_:at_ + P] for v in w], rhs(4 * h + k),
                                       start=(h == 0 and k == 0), stop=(h == 1 and k == 3))
                        if h == 1:
                            yield i, last

            def ssq(m, c0):
                if m == 0:
                    pe.wait_ge(table_in, 16)
                else:
                    pe.wait_ge(h_ready, KD * m + 1)
                for k in range(KD):
                    pe.wait_ge(sq_done, KD * m + k + 1)
                    last = mm(ps[:, ss_bank(m), 0:T - c0], c_("d_mean"), sq[:, k, c0:T], start=(k == 0), stop=(k == KD - 1))
                last.then_inc(ssq_ready, 1)

            pe.wait_ge(ident_in, 16)
            pe.wait_ge(x_in, 48)
            for i, (o, n) in enumerate(((0, META), (META, P), (META + P, P))):
                for h in range(2):
                    for k in range(4):
                        last = nc.tensor.transpose(ps[:, 2 * i + h, k * P:k * P + n], xt[0:n, i, (4 * h + k) * P:(4 * h + k + 1) * P],
                                                   ident[0:n, 0:n])
                    last.then_inc(xt_ready, 1)

            u = 0
            for l in range(DEPTH):
                c0 = c0_of(l)
                ssq(2 * l, 0)
                seq = 0
                if l == 0:
                    pe.wait_ge(xt_taken, 4)
                for g in range(13):
                    outs = [ps[:, (seq + i) % 4, 0:T] for i in range(2)]
                    if g >= 2:
                        pe.wait_ge(z_taken, 26 * l + seq - 2)
                    for i, last in column_pair(u, outs, tokens(0), None if g else lambda k: pe.wait_ge(n_ready, 2 * l * KD + k + 1)):
                        last.then_inc(z_ready, 1)
                    u += 2
                    seq += 2
                    if g == 3:
                        pe.wait_ge(small_in, 48 * (l + 1))
                        pe.wait_ge(lora_act, l + 1)
                        for j in range(NPAIR):
                            last = mm(ps[:, 4 + j, 0:T], lora_w[0:HD, j * P:(j + 1) * P], th2[0:HD, 0, :], start=True, stop=True)
                        last.then_inc(lora_ready, 1)
                    if g == 4:
                        pe.wait_ge(lora_mixed, l + 1)
                        pe.wait_ge(lora_taken, 2 * l + 1)
                        for j in range(NPAIR):
                            last = mm(ps[:, 4 + j, 0:T], lora_w[HD:P, j * P:(j + 1) * P], za[HD:P, 12, 1:T + 1], start=True, stop=True)
                        last.then_inc(lora_ready, 1)
                    if g == 5:
                        pe.wait_ge(kk_sq, l + 1)
                        pe.wait_ge(lora_taken, 2 * l + 2)
                        for j in range(NPAIR):
                            last = mm(ps[:, 4 + j, 0:T], c_("head_mean"), tm[5][:, j, :], start=True, stop=True)
                        last.then_inc(kk_ss, 1)
                pe.wait_ge(pooled, l + 1)
                pe.wait_ge(z_taken, 26 * (l + 1))
                for j in range(NPAIR):
                    last = mm(ps[:, j, 0:T], pool_wt[:, j * P:(j + 1) * P], zc[:, j, PADC:], start=True, stop=True)
                last.then_inc(pool_ready, 1)
                pe.wait_ge(bonus_in, l + 1)
                for j in range(NPAIR):
                    last = mm(ps[:, 4 + j, 0:T], c_("head_mean"), tm[5][:, j, :], start=True, stop=True)
                last.then_inc(bonus_ready, 1)

                pe.wait_ge(wkv_in, l + 1)
                pe.wait_ge(pool_taken, l + 1)
                pe.wait_ge(blocks_zero, l + 1)
                for c, g in ORDER:
                    o, n = CHUNKS[c]
                    b = c % 2
                    rows = 2 * n
                    kind = kind_of(g)
                    prev = before_in_bank(c, g)
                    if prev is not None:
                        taken(pe, l, *prev)
                    bank = ps[:, 4 * b + BANK[kind], :]
                    X, XT, NT, W = (cb(b, s, rows, rows) for s in (S_X, S_XT, S_NT, S_W))
                    V, B_, K_ = (cb(b, s, P, rows) for s in (S_V, S_B, S_K))
                    MAK = cb(b, S_MAK, rows, rows)
                    MRB, MRK = mr(b, 0, rows), mr(b, 1, rows)
                    R1, U = cb(b, S_XT, P, rows), cb(b, S_W, P, rows)
                    if g == "TN":
                        taken(pe, l, c, "M1")
                    elif kind == "W":
                        if g == "W1":
                            taken(pe, l, c, "TN")
                            pe.wait_ge(x_init, l * NCH + c + 1)
                        else:
                            taken(pe, l, c, f"P{int(g[1:]) - 1}")
                    elif kind == "P":
                        taken(pe, l, c, "W" + g[1:])
                        if g != "P1":
                            taken(pe, l, c, f"Q{int(g[1:]) - 1}")
                    elif g == "R":
                        taken(pe, l, c, "TV")
                        taken(pe, l, c, "M2")
                        if c > 0:
                            taken(pe, l, c - 1, "S")
                    elif g == "U":
                        taken(pe, l, c, "R")
                        taken(pe, l, c, f"P{levels(n)}")
                    elif g == "Y":
                        taken(pe, l, c, "U")
                    elif g == "S":
                        taken(pe, l, c, "TK")
                    for j in range(NPAIR):
                        if g == "M1":
                            last = mm(bank[0:rows, j * rows:(j + 1) * rows], block(bd_b, P, j, o, n), block(pair_ar, P, j, o, n), start=True, stop=True)
                        elif g == "M2":
                            last = mm(bank[0:rows, j * rows:(j + 1) * rows], block(bd_k, P, j, o, n), block(pair_ar, P, j, o, n), start=True, stop=True)
                        elif g in ("TB", "TK", "TV"):
                            src = {"TB": bd_b, "TK": bd_k, "TV": bd_v}[g]
                            last = nc.tensor.transpose(bank[0:rows, j * P:(j + 1) * P], block(src, P, j, o, n), ident)
                        elif g == "TN":
                            last = nc.tensor.transpose(bank[0:rows, j * rows:(j + 1) * rows], W[:, j, :], c_("ident", rows)[:, 0:rows])
                        elif kind == "W":
                            last = mm(bank[0:rows, j * rows:(j + 1) * rows], NT[:, j, :], X[:, j, :], start=True, stop=True)
                        elif kind == "P":
                            last = mm(bank[0:rows, j * rows:(j + 1) * rows], XT[:, j, :], W[:, j, :], start=True, stop=True)
                        elif kind == "Q":
                            last = mm(bank[0:rows, j * rows:(j + 1) * rows], W[:, j, :], XT[:, j, :], start=True, stop=True)
                        elif g == "R":
                            if c > 0:
                                mm(bank[0:rows, j * P:(j + 1) * P], block(bd_a, P, j, o, n), state[:, j, :], start=True, stop=False)
                            last = mm(bank[0:rows, j * P:(j + 1) * P], MAK[:, j, :], V[:, j, :], start=(c == 0), stop=True)
                        elif g == "U":
                            last = mm(bank[0:rows, j * P:(j + 1) * P], X[:, j, :], R1[:, j, :], start=True, stop=True)
                        elif g == "Y":
                            dst = bank[:, j * n:(j + 1) * n]
                            if c > 0:
                                mm(dst, state[:, j, :], block(pair_ar, P, j, o, n)[:, n:2 * n], start=True, stop=False)
                            mm(dst, U[:, j, :], MRB[:, j, :], start=(c == 0), stop=False)
                            last = mm(dst, V[:, j, :], MRK[:, j, :], start=False, stop=True)
                        else:
                            mm(bank[:, j * P:(j + 1) * P], B_[:, j, :], U[:, j, :], start=True, stop=False)
                            last = mm(bank[:, j * P:(j + 1) * P], K_[:, j, :], V[:, j, :], start=False, stop=True)
                    last.then_inc(w_prod, 1)
                for b in range(2):
                    for g in ("R", "U", "Y", "S"):
                        taken(pe, l, NCH - 1 - b, g)

                merge_i = 0
                for b, y in ((2, yC), (1, yB), (0, yA)):
                    if b == 1:
                        pe.wait_ge(yb_done, l + 1)
                    if b == 0:
                        pe.wait_ge(ya_done, l + 1)
                    for i in range(4):
                        if b == 2 and i == 0:
                            for j in range(NPAIR):
                                last = mm(ps[:, 4 + j, 0:T], c_("head_mean"), yA[:, j, :], start=True, stop=True)
                            last.then_inc(stat_ready, 1)
                        if b == 2 and i == 1:
                            pe.wait_ge(conv_done, l + 1)
                            pe.wait_ge(conv_pool, (l + 1) * CONV_POOL)
                            pe.wait_ge(stat_cen, 2 * l + 1)
                            for j in range(NPAIR):
                                last = mm(ps[:, 4, 0:T], c_("c_mean"), yB[:, j, :], start=(j == 0), stop=(j == NPAIR - 1))
                            last.then_inc(stat_ready, 1)
                        if b == 2 and i == 2:
                            pe.wait_ge(stat_sq, 2 * l + 1)
                            pe.wait_ge(stat_cen, 2 * l + 2)
                            for j in range(NPAIR):
                                last = mm(ps[:, 4 + j, 0:T], c_("head_mean"), tm[0][:, j, :], start=True, stop=True)
                            last.then_inc(stat_ready, 1)
                        if b == 2 and i == 3:
                            pe.wait_ge(stat_sq, 2 * l + 2)
                            pe.wait_ge(root_done, 5 * l + 3)
                            for j in range(NPAIR):
                                last = mm(ps[:, 4, 0:T], c_("c_mean"), tm[1][:, j, :], start=(j == 0), stop=(j == NPAIR - 1))
                            last.then_inc(stat_ready, 1)
                        if b == 1 and i == 0:
                            pe.wait_ge(root_done, 5 * l + 4)
                            pe.wait_ge(gd_done, l + 1)
                            for j in range(NPAIR):
                                last = mm(ps[:, 4 + j, 0:T], g2_w[:, j * P:(j + 1) * P], za[:, 13, 1:T + 1], start=True, stop=True)
                            last.then_inc(g_ready, 1)
                        w = open_unit(u).rearrange("p (k c) -> p k c", k=NPAIR)
                        for t in range(2):
                            if merge_i >= 1:
                                pe.wait_ge(merge_taken, 24 * l + 2 * merge_i - 1 + t)
                            for k in range(NPAIR):
                                mmu(ps[:, 2 * t, 0:T - c0], w[:, k, t * P:(t + 1) * P], y[:, k, c0:T], start=(k == 0), stop=(k == NPAIR - 1))
                        for t, last in column_pair(u + 1, [ps[:, 1, 0:T - c0], ps[:, 3, 0:T - c0]], tokens(c0)):
                            last.then_inc(merge_ready, 1)
                        u += 3
                        merge_i += 1
                pe.wait_ge(merge_taken, 24 * (l + 1))
                for i in range(4):
                    for t, last in column_pair(u, [ps[:, 2 * i, 0:T - c0], ps[:, 2 * i + 1, 0:T - c0]], tokens(c0),
                                               None if i else lambda k: pe.wait_ge(m_lo, KD * l + k + 1)):
                        last.then_inc(out_ready, 1)
                    u += 2
                ssq(2 * l + 1, c0)
                if l == 0:
                    for g in range(FT // 2):
                        b4 = 4 * (g % 2)
                        if g >= 2:
                            pe.wait_ge(hu_taken, 2 * (g - 1))
                        for t, last in column_pair(u, [ps[:, b4, 0:T], ps[:, b4 + 1, 0:T]], tokens(0),
                                                   None if g else lambda k: pe.wait_ge(n_ready, KD + k + 1)):
                            pass
                        for t, last in column_pair(u + 2, [ps[:, b4 + 2, 0:T], ps[:, b4 + 3, 0:T]], tokens(0)):
                            last.then_inc(hu_ready, 1)
                        u += 4
                    pe.wait_ge(hu_taken, FT)
                    for ft in range(FT):
                        pe.wait_ge(hid_lo, ft + 1)
                        w = open_unit(u)
                        for k in range(KD):
                            last = mm3(ps[:, k, 0:T], [v[:, k * P:(k + 1) * P] for v in w], hid_r[ft % 4], start=(ft == 0), stop=(ft == FT - 1))
                            if ft == FT - 1:
                                last.then_inc(down_ready, 1)
                        u += 1

            pe.wait_ge(n_f32, KD)
            pe.wait_ge(moe_in, 32)
            for tt in range(2):
                for k in range(KD):
                    last = mm(ps[:, 0, tt * E:(tt + 1) * E], nT[:, k, META + tt * P:META + (tt + 1) * P],
                              rout_w[:, k * E:(k + 1) * E], start=(k == 0), stop=(k == KD - 1))
            last.then_inc(logit_ready, 1)
            for i, src in ((1, hT), (0, nT)):
                if i == 0:
                    pe.wait_ge(lg_taken, 1)
                for tt in range(2):
                    for h in range(2):
                        for k in range(4):
                            last = nc.tensor.transpose(ps[:, 4 * i + 2 * tt + h, k * P:(k + 1) * P],
                                                       src[:, 4 * h + k, META + tt * P:META + (tt + 1) * P], ident)
                            if (i, tt, h, k) == (1, 0, 0, 0):
                                last.then_inc(split_used, 1)
                        last.then_inc(tr_ready, 1)
            pe.wait_ge(tr_taken, 8)
            pe.wait_ge(sel_ready, 1)
            mm(ps[:, 1, 0:E], c_("before"), sel[:, 0, :], start=True, stop=True)
            mm(ps[:, 1, E:2 * E], c_("ones"), sel[:, 0, :], start=True, stop=False)
            mm(ps[:, 1, E:2 * E], c_("before"), sel[:, 1, :], start=False, stop=True)
            mm(ps[:, 1, 2 * E:3 * E], c_("ones"), sel[:, 0, :], start=True, stop=False)
            mm(ps[:, 1, 2 * E:3 * E], c_("ones"), sel[:, 1, :], start=False, stop=True).then_inc(pos_ready, 1)
            pe.wait_ge(route_done, 1)

            def expert_pass(n, ahead=0):
                pe.wait_ge(pick_ready, n + ahead + 1)
                for tt in range(2):
                    last = nc.tensor.transpose(ps[:, 6, tt * P:(tt + 1) * P], pickw[:, tt, :], ident)
                last.then_inc(gather_ready, 1)
                for h in range(2):
                    for k in range(4):
                        for tt in range(2):
                            last = mm(ps[:, 4 + h, k * P:(k + 1) * P], ntok[:, tt, (4 * h + k) * P:(4 * h + k + 1) * P],
                                      pick[:, tt, :], start=(tt == 0), stop=(tt == 1))
                    last.then_inc(gather_ready, 1)
                xh, xl = xe_s

                def split_unit(i):
                    pe.wait_ge(e_split, n * FFN_UNITS + i + 1)
                    return wsplit[(E_SPLIT0 + i) % SPLITS]

                def hid_transpose(d):
                    pe.wait_ge(ehid_done, n * FG + d + 1)
                    if d >= 2:
                        pe.wait_ge(ehid_lo, n * FG + d - 1)
                    for t in range(2):
                        last = nc.tensor.transpose(ps[:, 2 + d % 2, t * P:(t + 1) * P], hid_t[:, (2 * d + t) * P:(2 * d + t + 1) * P], ident)
                    last.then_inc(ehid_tr, 1)

                for i in range(4 * FG):
                    g, (m, h) = i // 4, divmod(i % 4, 2)
                    if i == 4 * (FG - 1):
                        hid_transpose(0)
                    if i % 4 == 0 and g >= 2:
                        pe.wait_ge(ehid_done, n * FG + g - 1)
                    wh, wl = split_unit(i)
                    if i < 2:
                        pe.wait_ge(xe_lo_done, n * 2 + 1 + h)
                    if i == 0:
                        pe.wait_ge(scat_taken, n * 4 + 4)
                    dst = ps[:, 4 * m + g % 2, 0:256]
                    for k in range(4):
                        x_, c = slice((4 * h + k) * SLOTS, (4 * h + k + 1) * SLOTS), slice(k * 256, (k + 1) * 256)
                        mm(dst, xh[:, x_], wh[:, c], start=(h == 0 and k == 0), stop=False)
                        mm(dst, xh[:, x_], wl[:, c], start=False, stop=False)
                        last = mm(dst, xl[:, x_], wh[:, c], start=False, stop=(h == 1 and k == 3))
                    last.then_inc(split_used, 1)
                for ft in range(FT):
                    d = ft // 2
                    if ft % 2 == 0:
                        if d + 1 < FG:
                            hid_transpose(d + 1)
                        pe.wait_ge(ehid_lo, n * FG + d + 1)
                    if ft == 0:
                        pe.wait_ge(gather_taken, n * 3 + 1)
                    wh, wl = split_unit(4 * FG + ft)
                    hh, hl = (v[:, ft % 2 * P:(ft % 2 + 1) * P] for v in hid_s[d % 2])
                    for h in range(2):
                        c = slice(h * 512, (h + 1) * 512)
                        mm(ps[:, 6 + h, :], hh, wh[:, c], start=(ft == 0), stop=False)
                        mm(ps[:, 6 + h, :], hh, wl[:, c], start=False, stop=False)
                        last = mm(ps[:, 6 + h, :], hl, wh[:, c], start=False, stop=(ft == FT - 1))
                    last.then_inc(split_used, 1)
                for h in range(2):
                    pe.wait_ge(y_taken, n * 2 + h + 1)
                    for tt in range(2):
                        mm(ps[:, YBANK[tt, h], :], pickT[:, tt * P:(tt + 1) * P], ye[:, h * 512:(h + 1) * 512],
                           start=True, stop=True).then_inc(scat_ready, 1)

            with pe.Fori(0, E) as e:
                expert_pass(e)
            with pe.register("passes") as passes:
                pe.reg_mov(passes, E)
                for q in range(1, PASSES):
                    with pe.Fori(0, E) as e:
                        count = pe.value_load(count_i[0:1, bass.ds(e, 1)].bitcast(I32))
                        with pe.If(count > q * SLOTS):
                            expert_pass(pe.snap(passes), ahead=1)
                            pe.reg_add(passes, passes, 1)

        @blk.scalar
        def _(act):
            af = nc.scalar.activation
            act.dma_start(cf[:, 0:P], const_f[:, 0:P]).then_inc(ident_in, 16)
            act.dma_start(xt[0:META, 0, :], meta).then_inc(x_in, 16)
            act.dma_start(xt[:, 1, :], x[0, 0:P, :]).then_inc(x_in, 16)
            act.dma_start(xt[:, 2, :], x[0, P:2 * P, :]).then_inc(x_in, 16)
            act.dma_start(cf[:, P:], const_f[:, P:]).then_inc(table_in, 16)
            act.dma_start(par[:, :].rearrange("p (l c) -> p l c", l=DEPTH), params.rearrange("l p c -> p l c")).then_inc(const_in, 16)
            act.dma_start(taps[:, :].rearrange("p (l c) -> p l c", l=DEPTH), conv_w.rearrange("l p c -> p l c")).then_inc(const_in, 16)
            act.dma_start(stage, const_u).then_inc(masks_in, 16)

            rounded = [0]

            def rounds(upto):
                for u in range(rounded[0], min(upto, MOE_UNIT0)):
                    if u in RAW:
                        continue
                    q = split_at(u)
                    act.wait_ge(ring_in[u % RING], 16 * (u // RING + 1))
                    if q >= SPLITS:
                        act.wait_ge(split_used, q - SPLITS + 1)
                    af(wsplit[q % SPLITS][0], ring[:, (u % RING) * UNIT:(u % RING + 1) * UNIT], ACT.Copy).then_inc(w_hi, 1)
                rounded[0] = max(rounded[0], upto)

            def squares(m, c0, unit=None):
                n = 4 if m == 0 else 1
                for k in range(0, KD, n):
                    if unit is not None:
                        rounds(unit + k // 2 * 2 + 4)
                    act.wait_ge(h_ready, KD * m + k + n)
                    af(sq[:, k:k + n, c0:T], hT[:, k:k + n, c0:T], ACT.Square).then_inc(sq_done, n)
                act.wait_ge(ssq_ready, m + 1)
                af(nrm[:, c0:T], ps[:, ss_bank(m), 0:T - c0], ACT.Sqrt, bias=eps(0)).then_inc(root_done, 1)

            def eps(i):
                return c_("eps")[:, i:i + 1]

            act.wait_ge(table_in, 16)
            act.wait_ge(ident_in, 16)

            unit0 = 0
            for l in range(DEPTH):
                c0 = c0_of(l)
                if l > 0:
                    rounds(unit0 + 2)
                squares(2 * l, 0)
                act.wait_ge(const_in, 16 * CONST_DMAS)
                act.wait_ge(half_done, l + 1)
                act.wait_ge(prep_done, l + 1)
                for s, j in enumerate(Z_ORDER):
                    rounds(unit0 + s // 2 * 2 + 4)
                    act.wait_ge(z_ready, 26 * l + s + 1)
                    src = ps[:, s % 4, 0:T]
                    if j < A_TILES:
                        af(za[:, j, 1:T + 1], src, ACT.Copy).then_inc(z_taken, 1)
                    elif j < A_TILES + NPAIR:
                        af(glu[:, j - A_TILES, TAPS - 1:], src, ACT.Copy, scale=0.5).then_inc(z_taken, 1)
                    elif j < A_TILES + B_TILES:
                        af(yB[:, j - A_TILES - NPAIR, :], src, ACT.Tanh, scale=0.5).then_inc(z_taken, 1)
                    else:
                        af(zc[:, j - A_TILES - B_TILES, PADC:], src, ACT.Copy).then_inc(z_taken, 1)
                    if s == 5:
                        act.wait_ge(lora_mixed, l + 1)
                        af(th2[0:HD, 0, :], za[0:HD, 12, 1:T + 1], ACT.Tanh).then_inc(lora_act, 1)
                        af(za[:, 13, 1:T + 1], za[:, 13, 1:T + 1], ACT.Tanh, scale=0.5).then_inc(gd_tanh, 1)
                    if s == 7:
                        act.wait_ge(lora_ready, 2 * l + 1)
                        for j2 in range(NPAIR):
                            last = af(tm[0][:, j2, :], ps[:, 4 + j2, 0:T], ACT.Tanh, scale=0.5, bias=half[:, 24 + j2:25 + j2])
                        last.then_inc(lora_taken, 1)
                    if s == 9:
                        act.wait_ge(lora_ready, 2 * l + 2)
                        for j2 in range(NPAIR):
                            last = af(tm[4][:, j2, :], ps[:, 4 + j2, 0:T], ACT.Tanh, scale=0.5, bias=half[:, 28 + j2:29 + j2])
                        last.then_inc(lora_taken, 1)
                    if s == 12:
                        act.wait_ge(decay_log, l + 1)
                        af(tmp[2], tmp[2], ACT.Exp).then_inc(decay_exp, 1)
                        af(tmp[0], tmp[1], ACT.Exp, scale=-1.0).then_inc(decay_exp, 1)
                        act.wait_ge(decay_exp, 3 * l + 2)
                        af(tmp[1], tmp[1], ACT.Exp).then_inc(decay_exp, 1)
                    if s == 11:
                        act.wait_ge(kk_floor, l + 1)
                        af(tmp[5], tmp[5], ACT.Sqrt).then_inc(root_done, 1)
                act.wait_ge(pool_ready, l + 1)
                for j in range(NPAIR):
                    last = af(yC[:, j, :], ps[:, j, 0:T], ACT.Copy, scale=p_(l, "c_scale", j))
                last.then_inc(pool_taken, 1)

                unit0 += W_IN_UNITS
                rounds(unit0 + 3)
                for c, g in ORDER:
                    if taker(g) != "act":
                        continue
                    o, n = CHUNKS[c]
                    b = c % 2
                    rows = 2 * n
                    kind = kind_of(g)
                    act.wait_ge(w_prod, wkv_count(l, c, g))
                    bank = ps[:, 4 * b + BANK[kind], :]
                    if kind == "W":
                        if g == "W1":
                            act.wait_ge(x_init, l * NCH + c + 1)
                        dst, src = cb(b, S_W, rows, rows), bank[0:rows, 0:4 * rows]
                    elif g == "TN":
                        dst, src = cb(b, S_NT, rows, rows), bank[0:rows, 0:4 * rows]
                    elif g == "Y":
                        dst, src = yA[:, :, o:o + n], bank[:, 0:4 * n]
                    else:
                        slot_ = {"TB": S_B, "TK": S_K, "TV": S_V, "R": S_XT, "U": S_W}[g]
                        dst, src = cb(b, slot_, P, rows), bank[0:rows, :]
                    af(dst, src.rearrange("p (j c) -> p j c", j=NPAIR), ACT.Copy).then_inc(w_act, 1)

                act.wait_ge(stat_cen, 2 * l + 1)
                af(tmp[0], tmp[2], ACT.Square).then_inc(stat_sq, 1)
                act.wait_ge(conv_pool, (l + 1) * CONV_POOL)
                for i in range(24):
                    if i == 2:
                        act.wait_ge(stat_cen, 2 * l + 2)
                        af(tmp[1], tmp[3], ACT.Square).then_inc(stat_sq, 1)
                    if i == 4:
                        act.wait_ge(stat_ready, 4 * l + 3)
                        af(tm[4], ps[:, 4:8, 0:T], ACT.Sqrt, bias=eps(2)).then_inc(root_done, 1)
                    if i == 6:
                        act.wait_ge(stat_ready, 4 * l + 4)
                        af(nrm, ps[:, 4, 0:T], ACT.Sqrt, bias=eps(1)).then_inc(root_done, 1)
                        act.wait_ge(yb_lin, l + 1)
                        af(tmp[1], yB_flat, ACT.Tanh).then_inc(yb_tanh, 1)
                    rounds(unit0 + i // 2 * 3 + 5)
                    act.wait_ge(merge_ready, 24 * l + i + 1)
                    if i >= 2:
                        act.wait_ge(merge_taken, 24 * l + i - 1)
                    b = (2, 1, 0)[i // 8]
                    j = 8 * b + i % 8
                    af(th2[:, i % 2, c0:T], ps[:, 2 * (i % 2) + 1, 0:T - c0], ACT.Tanh, scale=0.5, bias=half[:, j:j + 1]).then_inc(gate_done, 1)
                for k in range(KD):
                    act.wait_ge(merge_taken, 24 * l + 17 + k)
                    af(xr[0][:, k, c0:T], merged[:, k, c0:T], ACT.Copy).then_inc(m_hi, 1)
                unit0 += 36
                squares(2 * l + 1, c0, unit0)
                unit0 += 8
                if l == 0:
                    for ft in range(FT):
                        rounds(unit0 + ft // 2 * 4 + 6)
                        act.wait_ge(hu_ready, ft + 1)
                        if ft >= 4:
                            act.wait_ge(hu_taken, ft - 3)
                        af(fth[:, ft % 4, :], ps[:, 4 * (ft // 2 % 2) + ft % 2, 0:T], ACT.Tanh, scale=0.5).then_inc(hu_gate, 1)
                    unit0 += 4 * FG
                    for ft in range(FT):
                        if ft < 4:
                            rounds(unit0 + min(ft, 1) + 1)
                        else:
                            rounds(unit0 + ft)
                            act.wait_ge(split_used, split_at(unit0) + ft - 3)
                        act.wait_ge(hu_taken, ft + 1)
                        af(hid_r[ft % 4][0], hid[:, ft, :], ACT.Copy).then_inc(hid_hi, 1)
                    rounds(unit0 + FT)
                    unit0 += FT
                    rounds(unit0 + 2)

            for i in range(4):
                act.wait_ge(tr_ready, i + 1)
                af(hres[:, i // 2, i % 2 * 512:(i % 2 + 1) * 512], ps[:, 4 + i, :], ACT.Copy).then_inc(tr_taken, 1)
            act.wait_ge(gap_ready, 1)
            af(mx[:, :, 3], mx[:, :, 2], ACT.Exp).then_inc(gap_exp, 1)
            for i in range(4):
                act.wait_ge(tr_ready, 5 + i)
                af(ntok[:, i // 2, i % 2 * 512:(i % 2 + 1) * 512], ps[:, i, :], ACT.Copy).then_inc(tr_taken, 1)
            act.wait_ge(route_done, 1)

            def expert_pass(n):
                def w_round(i):
                    act.wait_ge(split_used, n * FFN_UNITS + E_SPLIT0 + i - SPLITS + 1)
                    act.wait_ge(ering_in[i % ERING], 16 * (i // ERING + 1) + n * (16 * (FFN_UNITS // ERING)))
                    af(wsplit[(E_SPLIT0 + i) % SPLITS][0], eslots[i % ERING], ACT.Copy).then_inc(w_hi, 1)

                for i in range(SPLITS):
                    w_round(i)
                act.wait_ge(gather_ready, n * 3 + 1)
                af(pickT, ps[:, 6, 0:2 * P], ACT.Copy).then_inc(gather_taken, 1)
                for h in range(2):
                    act.wait_ge(gather_ready, n * 3 + 2 + h)
                    af(xe_s[0][:, h * 512:(h + 1) * 512], ps[:, 4 + h, :], ACT.Copy).then_inc(gather_taken, 1)
                for i in range(SPLITS, FFN_UNITS):
                    g, d = (i - 4) // 4, (i - 4 * FG) // 2
                    w_round(i)
                    if i % 4 == 0 and g < FG:
                        act.wait_ge(split_used, n * FFN_UNITS + E_SPLIT0 + 4 * g + 2)
                        af(eth[:, g % 2, :], ps[:, g % 2, 0:256], ACT.Tanh, scale=0.5).then_inc(egate_tanh, 1)
                    if d >= 0 and i % 2 == 0:
                        act.wait_ge(ehid_tr, n * FG + d + 1)
                        af(hid_s[d % 2][0], ps[:, 2 + d % 2, 0:256], ACT.Copy).then_inc(ehid_hi, 1)
                act.wait_ge(split_used, n * FFN_UNITS + E_SPLIT0 + FFN_UNITS)
                for h in range(2):
                    af(ye[:, h * 512:(h + 1) * 512], ps[:, 6 + h, :], ACT.Copy).then_inc(y_taken, 1)

            with act.Fori(0, E) as e:
                expert_pass(e)
            with act.register("passes") as passes:
                act.reg_mov(passes, E)
                for q in range(1, PASSES):
                    with act.Fori(0, E) as e:
                        count = act.value_load(count_i[0:1, bass.ds(e, 1)].bitcast(I32))
                        with act.If(count > q * SLOTS):
                            expert_pass(act.snap(passes))
                            act.reg_add(passes, passes, 1)
                act.wait_ge(scat_taken, act.snap(passes) * 4 + 4)
            for i in range(2):
                af(ye, hres[:, i, :], ACT.Square, accum_out=ssq[:, i:i + 1]).then_inc(fin_sq, 1)
                act.wait_ge(fin_sq, i + 1)
            for i in range(2):
                af(ssq[:, i:i + 1], ssq[:, i:i + 1], ACT.Sqrt, scale=1.0 / D, bias=eps(0)).then_inc(root_done, 1)

        @blk.vector
        def _(dve):
            v = nc.vector
            steps = [0]

            counts = {}
            latest = []

            def mark(semaphore, by=1):
                counts[semaphore.name] = counts.get(semaphore.name, 0) + by
                latest[:] = [semaphore, counts[semaphore.name]]

            def settle():
                dve.wait_ge(*latest)

            def op(ins):
                steps[0] += 1
                ins.then_inc(dve_step, 1)
                mark(dve_step)
                return steps[0]

            def link(ins):
                dve.wait_ge(dve_step, op(ins))

            def norm(m, g, l, c0):
                dve.wait_ge(root_done, 5 * l + (1 if m % 2 == 0 else 5))
                settle()
                link(v.reciprocal(nrm[:, c0:T], nrm[:, c0:T]))
                settle()
                for k in range(KD):
                    ins = v.scalar_tensor_tensor(nT[:, k, c0:T], hT[:, k, c0:T], p_(l, g, k), nrm[:, c0:T], ALU.mult, ALU.mult)
                    if m == 2 * DEPTH - 1:
                        ins.then_inc(n_f32, 1)
                        mark(n_f32)
                        continue
                    link(ins)
                    link(v.tensor_copy(xr[0][:, k, c0:T], nT[:, k, c0:T]))
                    v.tensor_tensor(xr[1][:, k, c0:T], nT[:, k, c0:T], xr[0][:, k, c0:T].bitcast(F32), ALU.subtract).then_inc(n_ready, 1)
                    mark(n_ready)

            for i, (o, n) in enumerate(((0, META), (META, P), (META + P, P))):
                for h in range(2):
                    dve.wait_ge(xt_ready, 2 * i + h + 1)
                    done = h_ready if i == 2 else xt_taken
                    v.tensor_copy(hT[:, 4 * h:4 * h + 4, o:o + n],
                                  ps[:, 2 * i + h, :].rearrange("p (k t) -> p k t", k=4)[:, :, 0:n]).then_inc(done, 4 if i == 2 else 1)
                    mark(done, 4 if i == 2 else 1)
            dve.wait_ge(h_ready, KD)
            dve.wait_ge(table_in, 16)
            dve.wait_ge(ident_in, 16)
            dve.wait_ge(const_in, 16 * CONST_DMAS)

            for l in range(DEPTH):
                c0 = c0_of(l)
                settle()
                link(v.tensor_scalar(half[:, :], par[:, l * NPAR:l * NPAR + 32], 0.5, None, ALU.mult))
                settle()
                link(v.tensor_scalar(half_b[:, :], par[:, l * NPAR + COLS["b_g"][0]:l * NPAR + COLS["b_b"][0] + NPAIR], 0.5, None, ALU.mult))
                settle()
                v.tensor_scalar(omka[:, :], p_(l, "ka"), -1.0, 1.0, ALU.mult, ALU.add).then_inc(half_done, 1)
                mark(half_done)
                norm(2 * l, "mix_g", l, 0)
                dve.wait_ge(half_done, l + 1)

                def mix(tiles, scratch):
                    a, n = tiles[0], len(tiles)
                    settle()
                    link(v.tensor_tensor(scratch[:, 0:n, :], za[:, a:a + n, 0:T], za[:, a:a + n, 1:T + 1], ALU.subtract))
                    settle()
                    for i, j in enumerate(tiles):
                        last = v.scalar_tensor_tensor(za[:, j, 1:T + 1], scratch[:, i, :], p_(l, "mu", j), za[:, j, 1:T + 1], ALU.mult, ALU.add)
                        if j != tiles[-1]:
                            op(last)
                    return last

                if l == 0:
                    dve.wait_ge(masks_in, 16)
                    v.tensor_copy(cu[:, :], stage).then_inc(masks_done, 1)
                    mark(masks_done)
                dve.wait_ge(z_taken, 26 * l + 2)
                mix([12, 13], tm[6]).then_inc(lora_mixed, 1)
                mark(lora_mixed)
                dve.wait_ge(z_taken, 26 * l + 6)
                link(mix([4, 5, 6, 7], tm[6]))
                settle()
                link(v.tensor_tensor(tm[3], zk, wide(p_(l, "kk"), T), ALU.mult))
                settle()
                v.tensor_tensor(tm[5], tm[3], tm[3], ALU.mult).then_inc(kk_sq, 1)
                mark(kk_sq)
                dve.wait_ge(gd_tanh, l + 1)
                settle()
                v.tensor_scalar(za[:, 13, 1:T + 1], za[:, 13, 1:T + 1], 1.0, 0.5, ALU.add, ALU.mult).then_inc(gd_done, 1)
                mark(gd_done)
                dve.wait_ge(z_taken, 26 * l + 10)
                op(mix([0, 1, 2, 3], tm[6]))
                dve.wait_ge(lora_taken, 2 * l + 1)
                dve.wait_ge(masks_done, 1)
                settle()
                link(v.tensor_scalar(tmp[0], tmp[0], 1.0, -0.5 * DECAY, ALU.add, ALU.mult))
                settle()
                link(v.tensor_tensor_scan(tmp[1], cu[:, CU_SCAN:CU_SCAN + NPAIR * T], tmp[0], 0.0, ALU.mult, ALU.add))
                settle()
                v.tensor_tensor(tmp[2], tmp[1], tmp[0], ALU.subtract).then_inc(decay_log, 1)
                mark(decay_log)
                dve.wait_ge(lora_taken, 2 * l + 2)
                settle()
                link(v.tensor_scalar(tmp[4], tmp[4], 1.0, 0.5, ALU.add, ALU.mult))
                settle()
                for j in range(NPAIR):
                    last = op(v.tensor_scalar(tm[6][:, j, :], tm[4][:, j, :], p_(l, "ka", j), omka[:, j:j + 1], ALU.mult, ALU.add))
                dve.wait_ge(dve_step, last)
                settle()
                link(v.tensor_tensor(tm[6], tm[6], zk, ALU.mult))
                dve.wait_ge(kk_ss, l + 1)
                settle()
                v.tensor_scalar(tm[5], ps[:, 4:8, 0:T], 1e-24 / HD, None, ALU.max).then_inc(kk_floor, 1)
                mark(kk_floor)
                dve.wait_ge(root_done, 5 * l + 2)
                settle()
                link(v.reciprocal(tmp[5], tmp[5]))
                settle()
                op(v.scalar_tensor_tensor(tmp[3], tmp[3], -(HD ** -0.5), tmp[5], ALU.mult, ALU.mult))
                settle()
                link(v.scalar_tensor_tensor(tmp[4], tmp[3], -1.0, tmp[4], ALU.mult, ALU.mult))
                settle()
                link(v.tensor_tensor(tm[5], tm[6], zr, ALU.mult))
                settle()
                v.tensor_tensor(tm[5], tm[5], wide(p_(l, "rk"), T), ALU.mult).then_inc(bonus_in, 1)
                mark(bonus_in)
                dve.wait_ge(z_taken, 26 * l + 14)
                op(mix([8, 9, 10, 11], mix_v))
                dve.wait_ge(decay_exp, 3 * l + 3)
                dve.wait_ge(blocks_zero, l + 1)
                settle()
                for c, (o, n) in enumerate(CHUNKS):
                    op(v.tensor_copy(chunk_decay[:, c, :], tm[1][:, :, o + n - 1]))
                settle()
                for o, n, k in SPANS:
                    for part, h in ((LOW, 0), (HIGH, 1)):
                        op(v.tensor_tensor(halves(bd_a, part, h, o, n, k), cols(tm[3], part, o, n, k), cols(tm[2], part, o, n, k), ALU.mult))
                        op(v.tensor_tensor(halves(bd_b, part, h, o, n, k), cols(tm[4], part, o, n, k), cols(tm[0], part, o, n, k), ALU.mult))
                        op(v.tensor_tensor(halves(bd_k, part, h, o, n, k), cols(tm[6], part, o, n, k), cols(tm[0], part, o, n, k), ALU.mult))
                        op(v.tensor_copy(halves(bd_v, part, h, o, n, k), cols(zv, part, o, n, k)))
                    op(v.tensor_tensor(halves(pair_ar, ALLP, 0, o, n, k), cols(tm[3], ALLP, o, n, k), cols(tm[2], ALLP, o, n, k), ALU.mult))
                    op(v.tensor_tensor(halves(pair_ar, ALLP, 1, o, n, k), cols(zr, ALLP, o, n, k), cols(tm[1], ALLP, o, n, k), ALU.mult))
                dve.wait_ge(z_taken, 26 * l + 18)
                W_ = T + PADC
                settle()
                link(v.tensor_tensor(pool1[:, 0:4, 1:W_], zc[:, 0:4, 1:W_], zc[:, 0:4, 0:W_ - 1], ALU.add))
                settle()
                link(v.tensor_tensor(pool2[:, 0:3, 3:W_], pool1[:, 1:4, 3:W_], pool1[:, 1:4, 1:W_ - 2], ALU.add))
                settle()
                link(v.tensor_tensor(pool1[:, 2:4, 7:W_], pool2[:, 1:3, 7:W_], pool2[:, 1:3, 3:W_ - 4], ALU.add))
                settle()
                link(v.tensor_tensor(pool2[:, 2, 15:W_], pool1[:, 3, 15:W_], pool1[:, 3, 7:W_ - 8], ALU.add))
                sums = [pool1[:, 0], pool2[:, 0], pool1[:, 2], pool2[:, 2]]
                settle()
                for j in range(4):
                    op(v.tensor_tensor(sums[j][:, PADC:2 * PADC], sums[j][:, PADC:2 * PADC], c_("inv_win")[:, 16 * j:16 * j + 16], ALU.mult))
                settle()
                for j in range(4):
                    op(v.scalar_tensor_tensor(zc[:, j, 2 * PADC:], sums[j][:, 2 * PADC:], 1.0 / (2 << j), zc[:, j, 2 * PADC:], ALU.mult, ALU.subtract))
                dve.wait_ge(dve_step, steps[0] - 1)
                settle()
                for j in range(4):
                    last = v.tensor_tensor(zc[:, j, PADC:2 * PADC], sums[j][:, PADC:2 * PADC], zc[:, j, PADC:2 * PADC], ALU.subtract)
                last.then_inc(pooled, 1)
                mark(pooled)
                settle()
                for j in range(NPAIR):
                    dve.wait_ge(z_taken, 26 * l + 23 + j)
                    last = op(v.scalar_tensor_tensor(glu[:, j, TAPS - 1:], yB[:, j, :], 1.0, glu[:, j, TAPS - 1:], ALU.add, ALU.mult))
                conv_last = [last] * NPAIR
                dve.wait_ge(bonus_ready, l + 1)
                settle()
                v.scalar_tensor_tensor(bonus, ps[:, 4:8, 0:T], float(HD), zv, ALU.mult, ALU.mult).then_inc(wkv_in, 1)
                mark(wkv_in)

                def conv(first, count):
                    for i in range(first, min(first + count, TAPS * CONV_DVE)):
                        k, j = divmod(i, CONV_DVE)
                        w = taps[:, l * NPAIR * TAPS + j * TAPS + k:][:, 0:1]
                        dve.wait_ge(dve_step, conv_last[j])
                        if k == 0:
                            ins = v.tensor_scalar(yB[:, j, :], glu[:, j, 0:T], w, p_(l, "conv_b", j), ALU.mult, ALU.add)
                        else:
                            ins = v.scalar_tensor_tensor(yB[:, j, :], glu[:, j, k:k + T], w, yB[:, j, :], ALU.mult, ALU.add)
                        if i == TAPS * CONV_DVE - 1:
                            ins.then_inc(conv_done, 1)
                            mark(conv_done)
                        else:
                            conv_last[j] = op(ins)

                tap = 0
                for c, g in ORDER:
                    if taker(g) != "dve" and g != "TN":
                        continue
                    o, n = CHUNKS[c]
                    b = c % 2
                    rows = 2 * n
                    kind = kind_of(g)
                    bank = ps[0:rows, 4 * b + BANK[kind], 0:4 * rows]
                    masks = (lambda lv: [cu[0:rows, (CU_64 if n == HD else CU_16) + (2 * lv + i) * rows:][:, 0:rows]
                                         .unsqueeze(1).broadcast_to([rows, NPAIR, rows]) for i in range(2)])
                    flat = (lambda ap: ap.rearrange("p (j c) -> p j c", j=NPAIR))
                    if g == "TN":
                        taken(dve, l, c, "TN")
                        dve.wait_ge(w_id, l * NCH + c + 1)
                        if c < 2:
                            dve.wait_ge(dve_step, steps[0])
                        taken(dve, l, c, "M1")
                        settle()
                        v.copy_predicated(cb(b, S_X, rows, rows), masks(0)[0], cb(b, S_W, rows, rows))
                        settle()
                        v.copy_predicated(cb(b, S_XT, rows, rows), masks(0)[1], cb(b, S_NT, rows, rows)).then_inc(x_init, 1)
                        mark(x_init)
                    else:
                        dve.wait_ge(w_prod, wkv_count(l, c, g))
                        if g in ("M1", "M2"):
                            q = bank.rearrange("p (j h n) -> p j h n", j=NPAIR, h=2)
                            strict = c_(f"strict{n}", rows).rearrange("p (h n) -> p h n", h=2).unsqueeze(1).broadcast_to([rows, NPAIR, 2, n])
                            incl = c_(f"incl{n}", rows).unsqueeze(1).broadcast_to([rows, NPAIR, n])
                            dst = cb(b, S_W if g == "M1" else S_MAK, rows, rows).rearrange("p j (h n) -> p j h n", h=2)
                            settle()
                            v.tensor_tensor(dst, q[:, :, 0:1, :].broadcast_to([rows, NPAIR, 2, n]), strict, ALU.mult)
                            settle()
                            v.tensor_tensor(mr(b, 0 if g == "M1" else 1, rows), q[:, :, 1, :], incl, ALU.mult).then_inc(w_dve, 1)
                            mark(w_dve)
                        elif kind in "PQ":
                            if g == "P1":
                                dve.wait_ge(x_init, l * NCH + c + 1)
                            i = 0 if kind == "P" else 1
                            settle()
                            v.copy_predicated(cb(b, (S_X, S_XT)[i], rows, rows), masks(int(g[1:]))[i], flat(bank)).then_inc(w_dve, 1)
                            mark(w_dve)
                        else:
                            full = flat(ps[:, 4 * b + BANK[kind], :])
                            if c > 0:
                                taken(dve, l, c - 1, "S")
                            settle()
                            link(v.tensor_tensor(state, state, full, ALU.add))
                            settle()
                            v.tensor_tensor(state, state, wide(chunk_decay[:, c, :], P), ALU.mult).then_inc(w_dve, 1)
                            mark(w_dve)
                    n_taps = 2 if kind in ("Q", "M2") else 1
                    conv(tap, n_taps)
                    tap += n_taps

                def merge(i):
                    j = i % KD
                    dve.wait_ge(merge_ready, 24 * l + i + 1)
                    dve.wait_ge(gate_done, 24 * l + i + 1)
                    prod = ps[:, 2 * (i % 2), 0:T - c0]
                    if i < KD:
                        settle()
                        v.scalar_tensor_tensor(merged[:, j, c0:T], th2[:, i % 2, c0:T], 1.0, prod, ALU.add, ALU.mult).then_inc(merge_taken, 1)
                        mark(merge_taken)
                    else:
                        settle()
                        link(v.scalar_tensor_tensor(th2[:, i % 2, c0:T], th2[:, i % 2, c0:T], 1.0, prod, ALU.add, ALU.mult))
                        if i % KD == 0:
                            dve.wait_ge(merge_taken, 24 * l + i)
                        settle()
                        v.tensor_tensor(merged[:, j, c0:T], merged[:, j, c0:T], th2[:, i % 2, c0:T], ALU.add).then_inc(merge_taken, 1)
                        mark(merge_taken)

                taken(dve, l, NCH - 1, "Y")
                dve.wait_ge(stat_ready, 4 * l + 1)
                settle()
                v.tensor_tensor(tm[2], yA, ps[:, 4:8, 0:T], ALU.subtract).then_inc(stat_cen, 1)
                mark(stat_cen)
                conv(tap, TAPS * CONV_DVE)
                merge(0)
                merge(1)
                dve.wait_ge(conv_done, l + 1)
                dve.wait_ge(conv_pool, (l + 1) * CONV_POOL)
                dve.wait_ge(stat_ready, 4 * l + 2)
                settle()
                v.tensor_tensor(tm[3], yB, ps[:, 4, 0:T].unsqueeze(1).broadcast_to([P, NPAIR, T]), ALU.subtract).then_inc(stat_cen, 1)
                mark(stat_cen)
                merge(2)
                merge(3)
                dve.wait_ge(root_done, 5 * l + 3)
                settle()
                def norm_a(j):
                    settle()
                    link(v.reciprocal(tm[4][:, j, :], tm[4][:, j, :]))
                    settle()
                    link(v.tensor_tensor(tm[2][:, j, :], tm[2][:, j, :], tm[4][:, j, :], ALU.mult))
                    settle()
                    link(v.tensor_scalar(tm[2][:, j, :], tm[2][:, j, :], p_(l, "lnx_w", j), p_(l, "lnx_b", j), ALU.mult, ALU.add))

                norm_a(0)
                norm_a(1)
                merge(4)
                merge(5)
                dve.wait_ge(root_done, 5 * l + 4)
                settle()
                link(v.reciprocal(nrm, nrm))
                settle()
                link(v.tensor_tensor(tm[3], tm[3], nrm.unsqueeze(1).broadcast_to([P, NPAIR, T]), ALU.mult))
                settle()
                for j in range(NPAIR):
                    last = v.tensor_scalar(yB[:, j, :], tm[3][:, j, :], half_b[:, j:j + 1], half_b[:, NPAIR + j:NPAIR + j + 1], ALU.mult, ALU.add)
                last.then_inc(yb_lin, 1)
                mark(yb_lin)
                dve.wait_ge(yb_lin, l + 1)
                dve.wait_ge(yb_tanh, l + 1)
                settle()
                v.scalar_tensor_tensor(yB_flat, tmp[1], 1.0, yB_flat, ALU.add, ALU.mult).then_inc(yb_done, 1)
                mark(yb_done)
                for j in range(2, 4):
                    merge(4 + j)
                    norm_a(j)
                settle()
                link(v.tensor_tensor(tm[2], tm[2], bonus, ALU.add))
                dve.wait_ge(g_ready, l + 1)
                settle()
                v.tensor_tensor(yA, tm[2], ps[:, 4:8, 0:T], ALU.mult).then_inc(ya_done, 1)
                mark(ya_done)
                for i in range(8, 24):
                    merge(i)
                for k in range(KD):
                    dve.wait_ge(m_hi, KD * l + k + 1)
                    settle()
                    v.tensor_tensor(xr[1][:, k, c0:T], merged[:, k, c0:T], xr[0][:, k, c0:T].bitcast(F32), ALU.subtract).then_inc(m_lo, 1)
                    mark(m_lo)
                settle()
                for i in range(KD):
                    dve.wait_ge(out_ready, KD * l + i + 1)
                    v.scalar_tensor_tensor(hT[:, i, c0:T], ps[:, i, 0:T - c0], 0.5, hT[:, i, c0:T], ALU.mult, ALU.add).then_inc(h_ready, 1)
                    mark(h_ready)
                dve.wait_ge(h_ready, KD * (2 * l + 2))
                norm(2 * l + 1, "ffn_g", l, c0)
                if l == 0:
                    for ft in range(FT):
                        b4 = 4 * (ft // 2 % 2) + ft % 2
                        dve.wait_ge(hu_gate, ft + 1)
                        settle()
                        link(v.scalar_tensor_tensor(ftm[:, ft % 2, :], fth[:, ft % 4, :], 1.0, ps[:, b4, 0:T], ALU.add, ALU.mult))
                        settle()
                        v.scalar_tensor_tensor(hid[:, ft, :], ftm[:, ft % 2, :], 0.5, ps[:, b4 + 2, 0:T], ALU.mult, ALU.mult).then_inc(hu_taken, 1)
                        mark(hu_taken)
                    for ft in range(FT):
                        dve.wait_ge(hid_hi, ft + 1)
                        settle()
                        v.tensor_tensor(hid_r[ft % 4][1], hid[:, ft, :], hid_r[ft % 4][0].bitcast(F32), ALU.subtract).then_inc(hid_lo, 1)
                        mark(hid_lo)
                    settle()
                    for k in range(KD):
                        dve.wait_ge(down_ready, k + 1)
                        v.tensor_tensor(hT[:, k, :], hT[:, k, :], ps[:, k, 0:T], ALU.add).then_inc(h_ready, 1)
                        mark(h_ready)
                    dve.wait_ge(h_ready, 3 * KD)

            settle()
            dve.wait_ge(moe_in, 32)
            dve.wait_ge(logit_ready, 1)
            both = lambda ap: ap.unsqueeze(2).broadcast_to([P, 2, E])
            settle()
            v.tensor_tensor(lg, ps[:, 0, 0:2 * E].rearrange("p (i e) -> p i e", i=2), rout_b[:, :].unsqueeze(1).broadcast_to([P, 2, E]), ALU.add).then_inc(lg_taken, 1)
            mark(lg_taken)

            def first_max(src, m, eq, first):
                settle()
                link(v.tensor_reduce(m, src, AX_X, ALU.max))
                settle()
                link(v.tensor_tensor(eq, src, both(m), ALU.is_equal))
                settle()
                for i in range(2):
                    last = op(v.tensor_tensor_scan(cnt1[:, i, :], c_("ones")[:, 0:E], eq[:, i, :], 0.0, ALU.mult, ALU.add))
                dve.wait_ge(dve_step, last)
                settle()
                link(v.scalar_tensor_tensor(first, cnt1, 1.0, eq, ALU.is_equal, ALU.mult))

            first_max(lg, mx[:, :, 0], eq1, first1)
            settle()
            link(v.scalar_tensor_tensor(lg2, first1, -1e30, lg, ALU.mult, ALU.add))
            first_max(lg2, mx[:, :, 1], eq2, first2)
            settle()
            v.tensor_tensor(mx[:, :, 2], mx[:, :, 1], mx[:, :, 0], ALU.subtract).then_inc(gap_ready, 1)
            mark(gap_ready)
            settle()
            v.tensor_tensor(sel, first1, first2, ALU.add).then_inc(sel_ready, 1)
            mark(sel_ready)
            dve.wait_ge(gap_exp, 1)
            settle()
            link(v.tensor_scalar(mx[:, :, 4], mx[:, :, 3], 1.0, None, ALU.add))
            settle()
            link(v.reciprocal(mx[:, :, 4], mx[:, :, 4]))
            settle()
            link(v.tensor_tensor(mx[:, :, 5], mx[:, :, 4], mx[:, :, 3], ALU.mult))
            settle()
            link(v.tensor_tensor(gw, first1, both(mx[:, :, 4]), ALU.mult))
            settle()
            link(v.tensor_tensor(lg2, first2, both(mx[:, :, 5]), ALU.mult))
            settle()
            op(v.tensor_tensor(gw, gw, lg2, ALU.add))
            dve.wait_ge(pos_ready, 1)
            dve.wait_ge(sel_ready, 1)
            settle()
            link(v.scalar_tensor_tensor(pos0, ps[:, 1, 0:2 * E].rearrange("p (i e) -> p i e", i=2), 1.0, sel, ALU.add, ALU.mult))
            settle()
            link(v.tensor_scalar(pos0, pos0, -1.0, None, ALU.add))
            settle()
            op(v.tensor_scalar(pos1, pos0, -float(SLOTS), None, ALU.add))
            for padded in (pos0x, gwx):
                settle()
                op(v.memset(padded[:, :, E:E + 1], -1.0))
            settle()
            v.tensor_copy(count_i.bitcast(I32), ps[:, 1, 2 * E:3 * E]).then_inc(route_done, 1)
            mark(route_done)
            settle()
            v.memset(ssq, 0.0).then_inc(scat_taken, 4)
            def picks(e, pos, gates):
                for tt in range(2):
                    v.tensor_scalar(pick[:, tt, :], c_("slot"), pos[:, tt, bass.ds(e, 1)], None, ALU.is_equal)
                for tt in range(2):
                    last = v.tensor_scalar(pickw[:, tt, :], c_("slot"), pos[:, tt, bass.ds(e, 1)], gates[:, tt, bass.ds(e, 1)], ALU.is_equal, ALU.mult)
                last.then_inc(pick_ready, 1)

            dve.wait_ge(dve_step, steps[0])
            dve.wait_ge(route_done, 1)
            dve.wait_ge(tr_taken, 8)
            picks(0, pos0x, gwx)

            def expert_pass(n, next_picks=None):
                def w_rest(i):
                    hi, lo = wsplit[(E_SPLIT0 + i) % SPLITS]
                    dve.wait_ge(w_hi, n * FFN_UNITS + E_SPLIT0 + i + 1)
                    v.tensor_tensor(lo, eslots[i % ERING], hi.bitcast(F32), ALU.subtract).then_inc(e_split, 1)

                w_rest(0)
                w_rest(1)
                for h in range(2):
                    dve.wait_ge(gather_taken, n * 3 + 2 + h)
                    c = slice(h * 512, (h + 1) * 512)
                    v.tensor_tensor(xe_s[1][:, c], ps[:, 4 + h, :], xe_s[0][:, c].bitcast(F32), ALU.subtract).then_inc(xe_lo_done, 1)
                for i in range(2, FFN_UNITS):
                    g, d = (i - 4) // 4, (i - 4 * FG) // 2
                    w_rest(i)
                    if i % 4 == 0 and g < FG:
                        dve.wait_ge(egate_tanh, n * FG + g + 1)
                        v.scalar_tensor_tensor(etm[:, g % 2, :], eth[:, g % 2, :], 1.0, ps[:, g % 2, 0:256], ALU.add, ALU.mult).then_inc(moe_step, 1)
                    if i % 4 == 2 and i >= 4 and g < FG:
                        dve.wait_ge(moe_step, n * FG + g + 1)
                        dve.wait_ge(split_used, n * FFN_UNITS + E_SPLIT0 + 4 * g + 4)
                        v.scalar_tensor_tensor(hid_t[:, g * 256:(g + 1) * 256], etm[:, g % 2, :], 0.5, ps[:, 4 + g % 2, 0:256],
                                               ALU.mult, ALU.mult).then_inc(ehid_done, 1)
                    if d >= 0 and i % 2 == 0:
                        dve.wait_ge(ehid_hi, n * FG + d + 1)
                        v.tensor_tensor(hid_s[d % 2][1], ps[:, 2 + d % 2, 0:256], hid_s[d % 2][0].bitcast(F32), ALU.subtract).then_inc(ehid_lo, 1)
                if next_picks is not None:
                    dve.wait_ge(xe_lo_done, n * 2 + 2)
                    picks(next_picks, pos0x, gwx)
                for h in range(2):
                    for tt in range(2):
                        dve.wait_ge(scat_ready, n * 4 + 2 * h + tt + 1)
                        part = hres[:, tt, h * 512:(h + 1) * 512]
                        v.tensor_tensor(part, part, ps[:, YBANK[tt, h], :], ALU.add).then_inc(scat_taken, 1)
                dve.wait_ge(scat_taken, n * 4 + 8)

            with dve.Fori(0, E) as e:
                expert_pass(e, e + 1)
            with dve.register("passes") as passes:
                dve.reg_mov(passes, E)
                for q in range(1, PASSES):
                    with dve.Fori(0, E) as e:
                        count = dve.value_load(count_i[0:1, bass.ds(e, 1)].bitcast(I32))
                        with dve.If(count > q * SLOTS):
                            picks(e, pos1, gw)
                            expert_pass(dve.snap(passes))
                            dve.reg_add(passes, passes, 1)
            for i in range(2):
                dve.wait_ge(root_done, 5 * DEPTH + 1 + i)
                dve.wait_ge(gain_in, 16)
                link(v.reciprocal(ssq[:, i:i + 1], ssq[:, i:i + 1]))
                v.scalar_tensor_tensor(ntok[:, i, :], hres[:, i, :], ssq[:, i:i + 1], fg, ALU.mult, ALU.mult).then_inc(fin_done, 1)


def kernel(**inputs):
    import concourse.bacc as bacc
    from concourse.bass_utils import run_bass_kernel_spmd

    a = {k: np.asarray(v) for k, v in inputs.items()}

    def channels(v):
        return np.transpose(v.reshape(DEPTH, -1, P), (0, 2, 1))

    names = dict(gate_b="gate_b", w0="a_w0", a0="a_a0", mix_g="mix_norm_g", mu="a_mu", kk="a_kk", ka="a_ka", rk="a_rk",
                 lnx_w="a_lnx_w", lnx_b="a_lnx_b", conv_b="b_conv_b", b_g="b_ln_g", b_b="b_ln_b", c_scale="c_scale", ffn_g="ffn_norm_g")
    const_f, const_u = constants()
    arrays = dict(
        x=a["x"], meta=a["meta_tokens"], w_in=a["w_in"],
        lora=np.concatenate([a["a_w2"], a["a_a2"]], 1), g2=a["a_g2"], pool_w=a["c_pool_w"],
        params=np.concatenate([channels(a[names[k]]) for k in COLS], 2),
        conv_w=np.ascontiguousarray(np.transpose(a["b_conv_w"].reshape(DEPTH, TAPS, NPAIR, P), (0, 3, 2, 1))).reshape(DEPTH, P, NPAIR * TAPS),
        proj_a=a["proj_a"], proj_b=a["proj_b"], proj_c=a["proj_c"], w_out=a["w_out"],
        ffn_gate=a["ffn_gate"], ffn_up=a["ffn_up"], ffn_down=a["ffn_down"], router_w=a["router_w"], router_b=a["router_b"],
        exp_gate=a["exp_gate"], exp_up=a["exp_up"], exp_down=a["exp_down"], final_g=a["final_norm_g"],
        const_f=const_f, const_u=const_u)
    nc = bacc.Bacc("TRN2", target_bir_lowering=False, num_devices=1)
    given, args = {}, []
    for name, v in arrays.items():
        given[f"in_{name}"] = np.ascontiguousarray(v)
        args.append(nc.dram_tensor(f"in_{name}", v.shape, mybir.dt.from_np(v.dtype), kind="ExternalInput").ap())
    args.append(nc.dram_tensor("out_0", (1, SEQ, D), F32, kind="ExternalOutput").ap())
    build(nc, *args)
    r = run_bass_kernel_spmd(nc, [given], core_ids=[0])
    return r.results[0]["out_0"]
```
